# Optimizing a Trainium2 kernel written in Bass

```python
import jax, jax.numpy as jnp
from jax import lax
import numpy as np

D_MODEL = 1024
BATCH = 1
SEQ = 512
DEPTH = 2
DEC_BATCH = 1
DEC_SEQ = 32
PAST_LEN = 1024

CHUNK = 64
N_EVEN = (DEPTH + 1) // 2
N_ODD = DEPTH // 2
D_A = D_MODEL // 2
D_B = D_MODEL // 2
CONV_A_WIDTH = 31
POOL_WINDOWS = (2, 4, 8, 16)
N_POOL_GROUPS = len(POOL_WINDOWS)
D_POOL_GROUP = D_B // N_POOL_GROUPS
POOL_BUF = max(POOL_WINDOWS) - 1
D_IN_EVEN = 2 * D_A + D_B
D_C = D_MODEL
CONV_C_WIDTH = 3
PEER_HEADS = 8
PEER_NKEYS = 128
PEER_EXPERTS = PEER_NKEYS * PEER_NKEYS
PEER_TOPK = 16
PEER_DQ = 256
PEER_DHALF = PEER_DQ // 2
PEER_BLOCK = 128
N_MOD = 6
EPS = 1e-6

kernel_name = 'hybrid_conv_pool_peer_stream_step'

def rmsnorm(x, g):
    xf = x.astype(jnp.float32)
    y = xf * lax.rsqrt(jnp.mean(xf * xf, axis=-1, keepdims=True) + EPS)
    return (y * g.astype(jnp.float32)).astype(x.dtype)

def layernorm(x, g, b):
    xf = x.astype(jnp.float32)
    mu = jnp.mean(xf, axis=-1, keepdims=True)
    var = jnp.mean(jnp.square(xf - mu), axis=-1, keepdims=True)
    y = (xf - mu) * lax.rsqrt(var + EPS)
    return (y * g.astype(jnp.float32) + b.astype(jnp.float32)).astype(x.dtype)

def depthwise_causal_conv(ext, w):
    c = ext.shape[-1]
    return lax.conv_general_dilated(ext, w[:, None, :].astype(ext.dtype), window_strides=(1,),
                                    padding='VALID', dimension_numbers=('NWC', 'WIO', 'NWC'),
                                    feature_group_count=c)

def multiscale_pool(ext, pos0, t):
    p = POOL_BUF
    xf = ext.astype(jnp.float32)
    cs = jnp.concatenate([jnp.zeros_like(xf[:, :1]), jnp.cumsum(xf, axis=1)], axis=1)
    pos = pos0 + jnp.arange(t)
    outs = []
    for gi, w in enumerate(POOL_WINDOWS):
        sl = slice(gi * D_POOL_GROUP, (gi + 1) * D_POOL_GROUP)
        s = cs[:, p + 1:p + 1 + t, sl] - cs[:, p + 1 - w:p + 1 - w + t, sl]
        cnt = jnp.minimum(w, pos + 1).astype(jnp.float32)
        outs.append(s / cnt[None, :, None])
    return jnp.concatenate(outs, axis=-1).astype(ext.dtype)

def mix_even(h, prev_a, prev_b, pos0, w_in, dw_a, db_a, ln_g, ln_b, w_pool, pool_scale, w_out):
    bsz, t, _ = h.shape
    p = h @ w_in
    a_lin, a_gate, b_in = p[..., :D_A], p[..., D_A:2 * D_A], p[..., 2 * D_A:]
    a = a_lin * jax.nn.sigmoid(a_gate)
    ext_a = jnp.concatenate([prev_a, a], axis=1)
    a_conv = depthwise_causal_conv(ext_a, dw_a) + db_a
    a_out = jax.nn.silu(layernorm(a_conv, ln_g, ln_b))
    ext_b = jnp.concatenate([prev_b, b_in], axis=1)
    pooled = (multiscale_pool(ext_b, pos0, t) - b_in).reshape(bsz, t, N_POOL_GROUPS, D_POOL_GROUP)
    b_out = jnp.einsum('btgc,gcd->btgd', pooled, w_pool).reshape(bsz, t, D_B) * pool_scale
    y = jnp.concatenate([a_out, b_out], axis=-1) @ w_out
    return y, ext_a[:, -(CONV_A_WIDTH - 1):], ext_b[:, -POOL_BUF:]

def mix_odd(h, prev_c, w_in, dw_c, w_out):
    p = h @ w_in
    bg, cg, xt = p[..., :D_C], p[..., D_C:2 * D_C], p[..., 2 * D_C:]
    ext = jnp.concatenate([prev_c, cg * xt], axis=1)
    y = (bg * depthwise_causal_conv(ext, dw_c)) @ w_out
    return y, ext[:, -(CONV_C_WIDTH - 1):]

def peer(h, wq, k1, k2, u, v):
    bsz, t, d = h.shape
    m = bsz * t
    pad = (-m) % PEER_BLOCK
    blocks = jnp.pad(h.reshape(m, d), ((0, pad), (0, 0))).reshape(-1, PEER_BLOCK, d)

    def block_fn(hb):
        q = (hb @ wq).reshape(PEER_BLOCK, PEER_HEADS, PEER_DQ)
        s1 = jnp.einsum('phd,hkd->phk', q[..., :PEER_DHALF], k1)
        s2 = jnp.einsum('phd,hkd->phk', q[..., PEER_DHALF:], k2)
        v1, i1 = lax.top_k(s1, PEER_TOPK)
        v2, i2 = lax.top_k(s2, PEER_TOPK)
        cand = (v1[..., :, None] + v2[..., None, :]).reshape(PEER_BLOCK, PEER_HEADS, PEER_TOPK * PEER_TOPK)
        cidx = (i1[..., :, None] * PEER_NKEYS + i2[..., None, :]).reshape(PEER_BLOCK, PEER_HEADS, PEER_TOPK * PEER_TOPK)
        sc, sel = lax.top_k(cand, PEER_TOPK)
        eidx = jnp.take_along_axis(cidx, sel, axis=-1)
        g = jax.nn.softmax(sc.astype(jnp.float32), axis=-1).astype(hb.dtype)
        act = jax.nn.gelu(jnp.einsum('phkd,pd->phk', u[eidx], hb))
        return jnp.einsum('phk,phkd->pd', g * act, v[eidx])

    out = lax.map(block_fn, blocks).reshape(-1, d)[:m]
    return out.reshape(bsz, t, d)

def run_trunk(x, c, prev_a, prev_b, prev_c, pos0, norm_mix_g, norm_ffn_g, w_ada, b_ada,
              w_in_even, dw_a, db_a, ln_a_g, ln_a_b, w_pool, pool_scale, w_out_even,
              w_in_odd, dw_c, w_out_odd, peer_wq, peer_k1, peer_k2, peer_u, peer_v, final_g):
    new_a, new_b, new_c = [], [], []
    c_act = jax.nn.silu(c)
    for l in range(DEPTH):
        mod = c_act @ w_ada[l] + b_ada[l]
        sh1, sc1, g1, sh2, sc2, g2 = [mm[:, None, :] for mm in jnp.split(mod, N_MOD, axis=-1)]
        h = rmsnorm(x, norm_mix_g[l]) * (1 + sc1) + sh1
        i = l // 2
        if l % 2 == 0:
            y, sa, sb = mix_even(h, prev_a[i], prev_b[i], pos0, w_in_even[i], dw_a[i], db_a[i],
                                 ln_a_g[i], ln_a_b[i], w_pool[i], pool_scale[i], w_out_even[i])
            new_a.append(sa)
            new_b.append(sb)
        else:
            y, scc = mix_odd(h, prev_c[i], w_in_odd[i], dw_c[i], w_out_odd[i])
            new_c.append(scc)
        x = x + g1 * y
        h = rmsnorm(x, norm_ffn_g[l]) * (1 + sc2) + sh2
        x = x + g2 * peer(h, peer_wq[l], peer_k1[l], peer_k2[l], peer_u[l], peer_v[l])
    return rmsnorm(x, final_g), jnp.stack(new_a), jnp.stack(new_b), jnp.stack(new_c)

def setup_inputs(seed: int = 0) -> dict:
    key = jax.random.key(seed)
    ks = jax.random.split(key, 32)
    f32 = jnp.float32

    def nrm(k, shape, scale):
        return jax.random.normal(k, shape, f32) * scale

    return {
        'x_prompt': nrm(ks[0], (BATCH, SEQ, D_MODEL), 1.0),
        'x_sample': nrm(ks[1], (DEC_BATCH, DEC_SEQ, D_MODEL), 1.0),
        'state_conv_a': nrm(ks[2], (N_EVEN, DEC_BATCH, CONV_A_WIDTH - 1, D_A), 0.5),
        'state_pool_b': nrm(ks[3], (N_EVEN, DEC_BATCH, POOL_BUF, D_B), 0.5),
        'state_conv_c': nrm(ks[4], (N_ODD, DEC_BATCH, CONV_C_WIDTH - 1, D_C), 0.5),
        'c_prompt': nrm(ks[5], (BATCH, D_MODEL), 1.0),
        'c_sample': nrm(ks[6], (DEC_BATCH, D_MODEL), 1.0),
        'norm_mix_g': 1.0 + nrm(ks[7], (DEPTH, D_MODEL), 0.05),
        'norm_ffn_g': 1.0 + nrm(ks[8], (DEPTH, D_MODEL), 0.05),
        'w_ada': nrm(ks[9], (DEPTH, D_MODEL, N_MOD * D_MODEL), 0.5 * D_MODEL ** -0.5),
        'b_ada': nrm(ks[10], (DEPTH, N_MOD * D_MODEL), 0.02),
        'w_in_even': nrm(ks[11], (N_EVEN, D_MODEL, D_IN_EVEN), D_MODEL ** -0.5),
        'dw_a': nrm(ks[12], (N_EVEN, CONV_A_WIDTH, D_A), CONV_A_WIDTH ** -0.5),
        'db_a': nrm(ks[13], (N_EVEN, D_A), 0.02),
        'ln_a_g': 1.0 + nrm(ks[14], (N_EVEN, D_A), 0.05),
        'ln_a_b': nrm(ks[15], (N_EVEN, D_A), 0.02),
        'w_pool': nrm(ks[16], (N_EVEN, N_POOL_GROUPS, D_POOL_GROUP, D_POOL_GROUP), D_POOL_GROUP ** -0.5),
        'pool_scale': 1.0 + nrm(ks[17], (N_EVEN, D_B), 0.1),
        'w_out_even': nrm(ks[18], (N_EVEN, D_A + D_B, D_MODEL), (D_A + D_B) ** -0.5),
        'w_in_odd': nrm(ks[19], (N_ODD, D_MODEL, 3 * D_C), D_MODEL ** -0.5),
        'dw_c': nrm(ks[20], (N_ODD, CONV_C_WIDTH, D_C), CONV_C_WIDTH ** -0.5),
        'w_out_odd': nrm(ks[21], (N_ODD, D_C, D_MODEL), D_C ** -0.5),
        'peer_wq': nrm(ks[22], (DEPTH, D_MODEL, PEER_HEADS * PEER_DQ), D_MODEL ** -0.5),
        'peer_k1': nrm(ks[23], (DEPTH, PEER_HEADS, PEER_NKEYS, PEER_DHALF), PEER_DHALF ** -0.5),
        'peer_k2': nrm(ks[24], (DEPTH, PEER_HEADS, PEER_NKEYS, PEER_DHALF), PEER_DHALF ** -0.5),
        'peer_u': nrm(ks[25], (DEPTH, PEER_EXPERTS, D_MODEL), D_MODEL ** -0.5),
        'peer_v': nrm(ks[26], (DEPTH, PEER_EXPERTS, D_MODEL), PEER_HEADS ** -0.5),
        'final_g': 1.0 + nrm(ks[27], (D_MODEL,), 0.05),
    }

def reference(x_prompt, x_sample, state_conv_a, state_pool_b, state_conv_c, c_prompt, c_sample,
              norm_mix_g, norm_ffn_g, w_ada, b_ada, w_in_even, dw_a, db_a, ln_a_g, ln_a_b,
              w_pool, pool_scale, w_out_even, w_in_odd, dw_c, w_out_odd,
              peer_wq, peer_k1, peer_k2, peer_u, peer_v, final_g):
    bp = x_prompt.shape[0]
    dt = x_prompt.dtype
    zero_a = jnp.zeros((N_EVEN, bp, CONV_A_WIDTH - 1, D_A), dt)
    zero_b = jnp.zeros((N_EVEN, bp, POOL_BUF, D_B), dt)
    zero_c = jnp.zeros((N_ODD, bp, CONV_C_WIDTH - 1, D_C), dt)
    y_prompt, pa_a, pa_b, pa_c = run_trunk(
        x_prompt, c_prompt, zero_a, zero_b, zero_c, 0, norm_mix_g, norm_ffn_g, w_ada, b_ada,
        w_in_even, dw_a, db_a, ln_a_g, ln_a_b, w_pool, pool_scale, w_out_even,
        w_in_odd, dw_c, w_out_odd, peer_wq, peer_k1, peer_k2, peer_u, peer_v, final_g)
    y_sample, sa_a, sa_b, sa_c = run_trunk(
        x_sample, c_sample, state_conv_a, state_pool_b, state_conv_c, PAST_LEN, norm_mix_g, norm_ffn_g,
        w_ada, b_ada, w_in_even, dw_a, db_a, ln_a_g, ln_a_b, w_pool, pool_scale, w_out_even,
        w_in_odd, dw_c, w_out_odd, peer_wq, peer_k1, peer_k2, peer_u, peer_v, final_g)
    return (y_prompt, y_sample, pa_a, pa_b, pa_c, sa_a, sa_b, sa_c)


_drawn_inputs = setup_inputs


def setup_inputs(seed=0):
    import zlib

    import numpy as np

    out = dict(_drawn_inputs(seed))
    spreads = {}
    factors = {'state_pool_b': 4.306,
     'db_a': 6.307,
     'ln_a_g': 4.324,
     'ln_a_b': 7.647,
     'norm_ffn_g': 3.044}
    for name, (base, spread) in spreads.items():
        noise = np.random.default_rng([zlib.crc32(name.encode()), seed]).standard_normal(out[name].shape)
        drawn = base * np.exp(spread * noise) if base else spread * noise
        out[name] = __import__('jax').numpy.asarray(drawn.astype(out[name].dtype))
    for name, factor in factors.items():
        out[name] = (out[name] * factor).astype(out[name].dtype)
    return out
```

```python
from contextlib import ExitStack, contextmanager

import numpy as np

import concourse.bass as bass
from concourse import mybir

ALU = mybir.AluOpType
ACT = mybir.ActivationFunctionType
AX = mybir.AxisListType
F32 = mybir.dt.float32
F16 = mybir.dt.float16
U32 = mybir.dt.uint32

P = 128
D = 1024
KD = D // P
LAYERS = 2
NP_, NS_ = 512, 32
T = NP_ + NS_
HALF = T // 2
DA = 512
KA = DA // P
WA, WC = 31, 3
WINDOWS = (2, 4, 8, 16)
PB = max(WINDOWS) - 1
HEADS, NKEYS, TOPK = 8, 128, 16
NQ = 2 * HEADS
EPS = 1e-6
NEG = float(np.float32(-3.0e38))

SLOT = 4096
RING = 4
PAIRS = 4
U_SCALE, W_SCALE = 32.0, 16.0
GROUPS = NKEYS // 4
BODIES = GROUPS // 2
SUB = 8
STEP = 32
ADA_SLOTS, IN_SLOTS, OUT_SLOTS, Q_SLOTS = 12, (3, 6), 2, 4
FRONT = tuple(ADA_SLOTS + IN_SLOTS[l] + OUT_SLOTS + Q_SLOTS for l in range(LAYERS))

EA_PAD, EB_PAD, EC_PAD = WA - 1, PB, WC - 1
EA_W, EB_W, EC_W = T + 2 * EA_PAD, T + 2 * EB_PAD, T + 2 * EC_PAD

VECTORS = [("norm_mix_g", LAYERS * KD), ("norm_ffn_g", LAYERS * KD), ("b_ada", LAYERS * 6 * KD), ("db_a", KA),
           ("ln_a_g", KA), ("ln_a_b", KA), ("pool_scale", KA), ("final_g", KD), ("dw_a", KA * WA),
           ("dw_c", KD * WC), ("c", KD * 2)]
VEC_AT = {}
VEC_N = 0
for _name, _n in VECTORS:
    VEC_AT[_name] = (VEC_N, _n)
    VEC_N += _n


class Count:

    def __init__(self, n=0):
        self.n, self.turns = n, []

    def at(self, ahead=0):
        value = self.n + ahead
        for turn, per in self.turns:
            value = turn * per + value
        return value

    def over(self, by):
        value = self.n // by
        for turn, per in self.turns:
            value = turn * (per // by) + value
        return value


@contextmanager
def loop(eng, times, *steps):
    with eng.Fori(0, times) as turn:
        starts = [c.n for c, _ in steps]
        for c, per in steps:
            c.turns.append((turn, per))
        yield turn
        for (c, per), start in zip(steps, starts):
            c.turns.pop()
            assert c.n - start == per, (c.n - start, per)
            c.n = start + per * times


class Walk:

    def __init__(self):
        self.use, self.act, self.dve = Count(), Count(), Count()

    def take(self, reader, n=1):
        self.use.n += n
        (self.act if reader == "act" else self.dve).n += n
        return self.use.n - 1

    def steps(self, act=0, dve=0):
        return (self.use, act + dve), (self.act, act), (self.dve, dve)


def _schedule():
    use = act = 0
    last, gate_act, expert_use, expert_act = [], [], [], []
    for l in range(LAYERS):
        last += [use + s + 1 for s in range(ADA_SLOTS)]
        use += ADA_SLOTS + 1
        last += [use + 4 * (s + 1) for s in range(IN_SLOTS[l])]
        use += 4 * IN_SLOTS[l]
        act += (12, 16)[l]
        if l == 0:
            use += KA + 2
            act += KA
        last += [use + 4 * (s + 1) for s in range(OUT_SLOTS)]
        use += 4 * OUT_SLOTS + 1
        last += [use + 4 * (s + 1) for s in range(Q_SLOTS)]
        use += NQ
        act += NQ
        gate_act.append(act)
        use += 5 * 8 + (T // STEP) * 8
        act += 5 * 6 + (T // STEP) * 8
        expert_use.append(use)
        expert_act.append(act)
        use += 12 * GROUPS
        act += 4 * GROUPS
    return last, gate_act, expert_use, expert_act


LAST_USE, GATE_ACT, EXPERT_USE, EXPERT_ACT = _schedule()
TILE_LINKS = 11


def build(nc, xT, vectors, state_a, state_b, state_c, w_pool, keys, front_w, U, V,
          out_y, out_ap, out_as, out_bp, out_bs, out_cp, out_cs, gates_dram):
    with ExitStack() as ctx:
        def sb(name, shape, dt=F32):
            return ctx.enter_context(nc.sbuf_tensor(name, shape, dt))

        def sem(name):
            return ctx.enter_context(nc.semaphore(name))

        X = sb("X", [P, KD, T])
        H = sb("H", [P, KD, T])
        ACCF = sb("ACC", [P, KD * T])
        ACC = ACCF[:, :].rearrange("p (k t) -> p k t", k=KD)
        Z = ACC
        ring = sb("ring", [P, RING, SLOT])
        keyT = sb("keyT", [P, NQ, NKEYS])
        vec = sb("vec", [P, VEC_N])
        wpool = sb("wpool", [P, KA, P])
        ones = sb("ones", [P, P])
        ident = sb("ident", [P, P])
        iota = sb("iota", [P, P])
        head_mask = sb("head_mask", [P, HEADS])
        inv_count = sb("inv_count", [P, PB + 1])
        mod = sb("mod", [P, LAYERS, 6 * KD, 2])
        scale = sb("scale", [P, LAYERS, 2, KD, 2])
        cact = sb("cact", [P, KD, 2])
        stat = sb("stat", [P, 3, T])
        carrier = sb("carrier", [P, 4])
        arena = sb("arena", [P, 18176])

        def part(at, *shape, dt=F32):
            n = int(np.prod(shape))
            assert at + n <= 18176, at + n
            v = arena[:, at:at + n]
            if dt is not F32:
                v = v.bitcast(dt)
            names = "abcd"[:len(shape)]
            if len(shape) > 1:
                sizes = {k: s for k, s in zip(names, shape)}
                v = v.rearrange(f"p ({' '.join(names)}) -> p {' '.join(names)}", **sizes)
            return v

        def vecs(name):
            at, n = VEC_AT[name]
            return vec[:, at:at + n]

        EA = part(0, KA, EA_W)
        EB = part(2416, KA, EB_W)
        CONV = part(4712, KA, EB_W)
        YC = part(7008, KA, T)
        SQ = part(9184, KA, T)
        PL = part(11360, KA, T)
        SG = part(13536, 2, T)
        PT = part(14624, 2, EB_W)
        BG = part(0, KD, T)
        EC = part(4352, KD, EC_W)
        YO = part(8736, KD, EC_W)
        QT = part(0, NQ, T)
        CAND = part(8704, HEADS, TOPK * TOPK)
        GG = part(8704, TOPK, P)
        ZAP = part(10752, HEADS, TOPK * TOPK)
        ZT = part(10752, NQ, NKEYS)
        GT = part(10752, TOPK, P)
        IT = part(12800, 2, P)
        BD = part(13056, SUB, HEADS, TOPK)
        O2 = part(14080, SUB, P)
        O1 = part(15104, 2, SUB, P)
        ROWS = part(17152, SUB, P)
        small = stat[:, :, :].rearrange("p a t -> p (a t)")
        V16 = small[:, 0:256].rearrange("p (h j k) -> p h j k", h=HEADS, j=2)
        I16 = small[:, 256:512].bitcast(U32).rearrange("p (h j k) -> p h j k", h=HEADS, j=2)
        IF = small[:, 512:768].rearrange("p (j h k) -> p j h k", j=2, h=HEADS)
        C8 = small[:, 768:896].rearrange("p (h k) -> p h k", h=HEADS)
        ZS = small[:, 896:904]
        RZ = small[:, 904:912]
        stage = ACCF[:, 0:4096].rearrange("p (s g t e) -> p s g t e", s=2, g=BODIES, t=16)
        H16 = part(0, KD * T).bitcast(F16).rearrange("p (s k t) -> p s k t", s=2, k=KD)
        GB = arena[:, 4352:4352 + 2 * T * 8]
        WT = part(13056, 2 * 4 * T).bitcast(F16).rearrange("p (g s j t) -> p g s j t", g=2, s=2, j=4)
        AG = stat[:, 0:2, :]
        raw = {"U": ring[:, 0, :], "V": ring[:, 1, :]}
        parts = {x: ring[:, 2 + i, :].bitcast(F16).rearrange("p (s n) -> p s n", s=2) for i, x in enumerate("UV")}

        PS = ctx.enter_context(nc.psum_tensor("PS", [P, PAIRS, 1024], F32))

        vec_in, x_in, state_in, pool_in, keys_in = (sem(x) for x in "vec_in x_in state_in pool_in keys_in".split())
        slot_in = [sem(f"slot_in{i}") for i in range(RING)]
        mm_done = sem("mm_done")
        act_read = sem("act_read")
        dve_read = sem("dve_read")
        consts_made, pads_made, c_in = sem("consts_made"), sem("pads_made"), sem("c_in")
        c_sigmoid, cact_ready, mod_ready = sem("c_sigmoid"), sem("cact_ready"), sem("mod_ready")
        x_ready, sq_ready, std_ready, xn_ready, h_ready = (sem(x) for x in "x_ready sq_ready std_ready xn_ready h_ready".split())
        glu_ready, pooled, conv_ready, centered, ln_sig, z_ready = (
            sem(x) for x in "glu_ready pooled conv_ready centered ln_sig z_ready".split())
        shifted, exped, gates_ready = sem("shifted"), sem("exped"), sem("gates_ready")
        bd_ready, o1_ready, o2_ready = sem("bd_ready"), sem("o1_ready"), sem("o2_ready")
        g_written = [sem(f"g_written{i}") for i in range(2)]
        raw_in = {x: sem(f"{x}_in") for x in "UV"}
        high_made = {x: sem(f"{x}_high_made") for x in "UV"}
        split = {x: sem(f"{x}_split") for x in "UV"}
        h_high, h_split, wf_ready, w_high = sem("h_high"), sem("h_split"), sem("wf_ready"), sem("w_high")
        g_in, w_ready, acc_zero = sem("g_in"), sem("w_ready"), sem("acc_zero")
        dve_step, pool_step, y_ready, y_out, state_out = (sem(x) for x in "dve_step pool_step y_ready y_out state_out".split())

        SEG = ((0, NP_, 0), (NP_, T, 1))
        mod_at = {"sh1": 0, "sc1": 1, "g1": 2, "sh2": 3, "sc2": 4, "g2": 5}
        CONSTS = 6
        NORM = (0, KD + KA, 2 * KD + KA, 3 * KD + KA, 4 * KD + KA)
        ORDER = ((1, 0), (1, 1), (2, 0), (1, 2), (2, 1), (1, 3), (2, 2), (2, 3))
        M1, M2 = (0, 1, 3, 5), (2, 4, 6, 7)
        STEPS = T // STEP
        PASSES = ((0, 0), (0, 1), (1, 0))

        def ps(u, n=T):
            return PS[:, u % PAIRS, 0:n]

        def ps_halves(u):
            return PS[:, u % PAIRS, :].rearrange("p (b c) -> p b c", b=2)[:, :, 0:HALF]

        block = ctx.enter_context(nc.Block())

        @block.sync
        def _(sp):
            def load(f):
                if f == FRONT[0] + (-FRONT[0]) % RING or f == FRONT[0] + (1 - FRONT[0]) % RING:
                    sp.wait_ge(split["UV"[f % RING]], GROUPS)
                elif FRONT[0] <= f < FRONT[0] + RING:
                    sp.wait_ge(mm_done, EXPERT_USE[0] + 12 * GROUPS)
                elif f >= RING:
                    sp.wait_ge(mm_done, LAST_USE[f - RING])
                sp.dma_start(ring[:, f % RING, :], front_w[f]).then_inc(slot_in[f % RING], 16)

            def load_raw(x, src):
                sp.dma_start(raw[x], src).then_inc(raw_in[x], 16)

            sp.dma_start(vec[:, :], vectors).then_inc(vec_in, 16)
            sp.dma_start(X[:, :, :], xT).then_inc(x_in, 16)
            f = 0
            view = gates_dram.rearrange("p g t e -> g p (t e)")
            for s in range(2):
                sp.sem_inc(g_written[s], 16)
            for l in range(LAYERS):
                while f < sum(FRONT[:l + 1]):
                    load(f)
                    f += 1
                    if f == sum(FRONT[:l]) + ADA_SLOTS:
                        sp.dma_start(keyT[:, :, :], keys[l]).then_inc(keys_in, 16)
                for i, x in enumerate("UV"):
                    sp.wait_ge(mm_done, LAST_USE[max(k for k in range(f) if k % RING == i)])
                    load_raw(x, (U, V)[i][l, 0])
                def spill(tile, step, bodies):
                    for s in range(2):
                        sp.wait_ge(act_read, step * 8 + tile * 38 + (GATE_ACT[l] + 6 + M2[2 * s + 1] + 1))
                        sp.dma_start(gates_dram[:, :, bass.ds(tile * P + step * STEP + 16 * s, 16), :],
                                     stage[:, s, :, :, :]).then_inc(g_written[s], 16)

                with sp.Fori(0, 4) as tile:
                    with sp.Fori(0, 4) as step:
                        spill(tile, step, 4)
                spill(4, 0, 1)
                for s in range(2):
                    sp.wait_ge(g_written[s], 16 * ((l + 1) * STEPS + 1))
                sp.wait_ge(mm_done, EXPERT_USE[l])
                sp.wait_ge(act_read, EXPERT_ACT[l])
                for k in range(2):
                    if k:
                        sp.wait_ge(g_in, 16 * (l * BODIES + k))
                    sp.dma_start(GB[:, k * T * 8:(k + 1) * T * 8], view[k]).then_inc(g_in, 16)
                def groups(body, n):
                    for k in range(n):
                        for x, src in (("U", U), ("V", V)):
                            sp.wait_ge(split[x], body * 2 + (l * GROUPS + k + 1))
                            if isinstance(body, int):
                                load_raw(x, src[l, 2 * body + k + 1])
                            else:
                                load_raw(x, src[l, bass.ds(body * 2 + (k + 1), 1)].rearrange("o p n -> (o p) n"))

                with sp.Fori(0, BODIES - 2) as body:
                    groups(body, 2)
                    sp.wait_ge(w_ready, body * 8 + (l * NKEYS + 10))
                    sp.wait_ge(g_in, body * 16 + 16 * (l * BODIES + 2))
                    sp.dma_start(GB[:, bass.ds((body % 2) * (T * 8), T * 8)],
                                 view[bass.ds(body + 2, 1)].rearrange("o p n -> (o p) n")).then_inc(g_in, 16)
                groups(BODIES - 2, 2)
                groups(BODIES - 1, 1)
            for k in range(KD):
                sp.wait_ge(y_ready, k + 1)
                sp.dma_start(out_y[:, k, :], H[:, k, :]).then_inc(y_out, 16)
            sp.wait_ge(y_out, 16 * KD)
            sp.wait_ge(state_out, 16 * 6)

        @block.tensor
        def _(pe):
            w, slot, wts, sub, group = Walk(), Count(), Count(2), Count(), Count()
            last = [None] * PAIRS

            def begin(reader):
                pair = w.use.n % PAIRS
                if last[pair] is not None:
                    who, value = last[pair]
                    pe.wait_ge(act_read if who == "act" else dve_read, value)
                u = w.take(reader)
                last[pair] = (reader, (w.act if reader == "act" else w.dve).at())
                return u

            def drained():
                for who, count in ((act_read, w.act), (dve_read, w.dve)):
                    if count.n:
                        pe.wait_ge(who, count.at())

            def from_turn_before(reader):
                count = w.act if reader == "act" else w.dve
                for i in range(PAIRS):
                    last[(w.use.n + i) % PAIRS] = (reader, count.at(i - PAIRS + 1))

            def slot_ready():
                pe.wait_ge(slot_in[slot.n % RING], slot.over(RING) * 16 + 16)
                slot.n += 1
                return ring[:, (slot.n - 1) % RING, :]

            def project(slots, src, readers, ready):
                for s in range(slots):
                    wt = slot_ready()
                    for m in range(4):
                        u = begin(readers[4 * s + m])
                        for k in range(KD):
                            if s == 0 and m == 0:
                                ready(k)
                            for a, b, _ in SEG:
                                mm = pe.matmul(ps(u)[:, a:b], wt[:, k * 512 + m * P:k * 512 + (m + 1) * P], src[:, k, a:b],
                                               start=(k == 0), stop=(k == KD - 1))
                        mm.then_inc(mm_done, 1)

            def column_sums(src, chunks, semaphore, value, gap=0):
                u = begin("dve")
                for k in range(chunks):
                    pe.wait_ge(semaphore, value + k)
                    for a, b, s in SEG:
                        mm = pe.matmul(ps(u)[:, a:b], ones[:, :], src[:, k, a + s * gap:b + s * gap],
                                       start=(k == 0), stop=(k == chunks - 1))
                mm.then_inc(mm_done, 1)

            def ada_slots():
                for _ in range(4):
                    wt = slot_ready()
                    u = begin("dve")
                    for m in range(4):
                        for k in range(KD):
                            mm = pe.matmul(ps(u)[:, 2 * m:2 * m + 2], wt[:, k * 512 + m * P:k * 512 + (m + 1) * P],
                                           cact[:, k, :], start=(k == 0), stop=(k == KD - 1))
                    mm.then_inc(mm_done, 1)

            pe.wait_ge(consts_made, CONSTS)
            pe.wait_ge(cact_ready, 1)
            for l in range(LAYERS):
                ada_slots()
                drained()
                with loop(pe, ADA_SLOTS // 4 - 1, *w.steps(dve=4), (slot, 4)):
                    from_turn_before("dve")
                    ada_slots()
                from_turn_before("dve")
                column_sums(H, KD, sq_ready, NORM[2 * l] + 1)
                project(IN_SLOTS[l], H, ["act"] * 12 if l == 0 else ["act"] * 16 + ["dve"] * 8,
                        lambda k: pe.wait_ge(h_ready, 2 * KD * l + k + 1))
                if l == 0:
                    pe.wait_ge(pool_in, 16)
                    for g in range(KA):
                        pe.wait_ge(pooled, g + 1)
                        u = begin("act")
                        for a, b, _ in SEG:
                            mm = pe.matmul(ps(u)[:, a:b], wpool[:, g, :], PL[:, g, a:b], start=True, stop=True)
                        mm.then_inc(mm_done, 1)
                    branch = w.act.at()
                    column_sums(CONV, KA, conv_ready, 1, EA_PAD)
                    column_sums(SQ, KA, sq_ready, KD + 1)
                    project(OUT_SLOTS, Z, ["dve"] * 8,
                            lambda k: pe.wait_ge(z_ready, k + 1) if k < KA else pe.wait_ge(act_read, branch))
                else:
                    project(OUT_SLOTS, Z, ["dve"] * 8, lambda k: pe.wait_ge(z_ready, KA + k + 1))
                column_sums(H, KD, sq_ready, NORM[2 * l + 1] + 1)
                project(Q_SLOTS, H, ["act"] * NQ, lambda k: pe.wait_ge(h_ready, 2 * KD * l + KD + k + 1))

                pe.wait_ge(keys_in, 16 * (l + 1))
                pe.wait_ge(act_read, w.act.at())
                for t in range(5):
                    n = P if t < 4 else NS_
                    for j in range(2):
                        u = begin("dve")
                        for q in range(8):
                            mm = pe.matmul(PS[0:n, u % PAIRS, q * P:(q + 1) * P], QT[:, 8 * j + q, t * P:t * P + n],
                                           keyT[:, 8 * j + q, :], start=True, stop=True)
                        mm.then_inc(mm_done, 1)
                    pe.wait_ge(gates_ready, l * 5 + t + 1)
                    for j in range(4):
                        u = begin("act")
                        for a in range(4):
                            mm = pe.transpose(ps(u, 512)[:, a * P:(a + 1) * P], GG[:, 4 * j + a, :], ident[:, :])
                        mm.then_inc(mm_done, 1)
                    for j in range(2):
                        u = begin("act")
                        pe.transpose(ps(u, P), IF[:, j, :, :].rearrange("p h k -> p (h k)"), ident[:, :]).then_inc(mm_done, 1)
                    drained()
                    with loop(pe, 4 if t < 4 else 1, *w.steps(act=8), (sub, 4)):
                        from_turn_before("act")
                        first = w.act.at()
                        r_count = [w.act.at(M1[s] + 1) for s in range(4)]
                        for which, s in ORDER:
                            u = begin("act")
                            if which == 1:
                                pe.wait_ge(bd_ready, sub.at(s + 1))
                                pe.wait_ge(o2_ready, sub.at(s + 1))
                                for i in range(SUB):
                                    mm = pe.matmul(ps(u, 1024)[:, i * P:(i + 1) * P],
                                                   BD[:, i, :, :].rearrange("p h k -> p (h k)"), O2[:, i, :],
                                                   start=True, stop=True)
                            else:
                                pe.wait_ge(o1_ready, sub.at(s + 1))
                                pe.wait_ge(act_read, r_count[s])
                                for i in range(SUB):
                                    mm = pe.matmul(ps(u, 1024)[:, i * P:(i + 1) * P], ROWS[:, i, :], O1[:, s % 2, i, :],
                                                   start=True, stop=True)
                            mm.then_inc(mm_done, 1)
                        sub.n += 4
                    from_turn_before("act")

                drained()
                pe.wait_ge(h_split, KD * (l + 1))
                with loop(pe, BODIES, *w.steps(act=8, dve=16), (group, 2), (wts, 8)):
                    from_turn_before("dve")
                    for grp in range(2):
                        pe.wait_ge(split["U"], group.at(1))
                        for j in range(4):
                            u = begin("act")
                            for k in range(KD):
                                for n, (pu, ph) in enumerate(PASSES):
                                    for half in range(2):
                                        mm = pe.matmul(ps_halves(u)[:, half, :], parts["U"][:, pu, k * 512 + j * P:k * 512 + (j + 1) * P],
                                                       H16[:, ph, k, half * HALF:(half + 1) * HALF],
                                                       start=(k == n == 0), stop=(k == KD - 1 and n == 2))
                            mm.then_inc(mm_done, 1)
                        pe.wait_ge(split["V"], group.at(1))
                        for c in range(KD):
                            u = begin("dve")
                            for j in range(4):
                                if c == 0:
                                    pe.wait_ge(w_ready, wts.at(j + 1))
                                for n, (pv, pw) in enumerate(PASSES):
                                    for half in range(2):
                                        mm = pe.matmul(ps_halves(u)[:, half, :], parts["V"][:, pv, j * D + c * P:j * D + (c + 1) * P],
                                                       WT[:, grp, pw, j, half * HALF:(half + 1) * HALF],
                                                       start=(j == n == 0), stop=(j == 3 and n == 2))
                            mm.then_inc(mm_done, 1)
                        wts.n += 4
                        group.n += 1
                from_turn_before("dve")
            column_sums(H, KD, sq_ready, NORM[4] + 1)

        @block.scalar
        def _(act):
            w, sub, body, wts, group = Walk(), Count(), Count(1), Count(2), Count()

            def next_use():
                act.wait_ge(mm_done, w.use.at(1))
                return w.take("act")

            def squares(src, dst, chunks, semaphore, value):
                for k in range(chunks):
                    act.wait_ge(semaphore, value + k)
                    act.activation(dst[:, k, :], src[:, k, :], ACT.Square).then_inc(sq_ready, 1)

            def root():
                w.take("dve")
                act.wait_ge(dve_read, w.dve.at())
                act.activation(stat[:, 1, :], stat[:, 0, :], ACT.Sqrt).then_inc(std_ready, 1)

            def modulate(l, which):
                sh = mod_at["sh1" if which == 0 else "sh2"] * KD
                for k in range(KD):
                    act.wait_ge(xn_ready, NORM[2 * l + which] + k + 1)
                    for a, b, s in SEG:
                        ins = act.activation(H[:, k, a:b], H[:, k, a:b], ACT.Identity,
                                             scale=scale[:, l, which, k, s:s + 1], bias=mod[:, l, sh + k, s:s + 1])
                    ins.then_inc(h_ready, 1)

            def store_state(dst, src):
                act.dma_start(dst, src).then_inc(state_out, 16)

            act.dma_start(EA[:, :, EA_PAD + NP_:2 * EA_PAD + NP_], state_a).then_inc(state_in, 16)
            act.dma_start(EB[:, :, EB_PAD + NP_:2 * EB_PAD + NP_], state_b).then_inc(state_in, 16)
            act.dma_start(wpool[:, :, :], w_pool).then_inc(pool_in, 16)
            act.wait_ge(vec_in, 16)
            act.activation(cact[:, :, :].rearrange("p k s -> p (k s)"), vecs("c"), ACT.Sigmoid).then_inc(c_sigmoid, 1)
            for l in range(LAYERS):
                w.take("dve", ADA_SLOTS)
                if l == 0:
                    act.wait_ge(x_in, 16)
                    for k in range(KD):
                        act.activation(H[:, k, :], X[:, k, :], ACT.Square).then_inc(sq_ready, 1)
                else:
                    squares(X, H, KD, x_ready, 1)
                root()
                act.wait_ge(mod_ready, l + 1)
                modulate(l, 0)
                if l == 0:
                    act.wait_ge(consts_made, CONSTS)
                    for c in range(KA):
                        u = next_use()
                        for a, b, s in SEG:
                            ins = act.copy(EA[:, c, a + EA_PAD * (1 + s):b + EA_PAD * (1 + s)], ps(u)[:, a:b])
                        ins.then_inc(act_read, 1)
                    for c in range(KA):
                        u = next_use()
                        if c >= 2:
                            act.wait_ge(glu_ready, c - 1)
                        act.activation(SG[:, c % 2, :], ps(u), ACT.Sigmoid).then_inc(act_read, 1)
                    for c in range(KA):
                        u = next_use()
                        for a, b, s in SEG:
                            ins = act.copy(EB[:, c, a + EB_PAD * (1 + s):b + EB_PAD * (1 + s)], ps(u)[:, a:b])
                        ins.then_inc(act_read, 1)
                    act.wait_ge(glu_ready, KA)
                    store_state(out_ap, EA[:, :, NP_:NP_ + EA_PAD])
                    store_state(out_as, EA[:, :, EA_W - EA_PAD:EA_W])
                    act.wait_ge(act_read, w.act.at())
                    store_state(out_bp, EB[:, :, NP_:NP_ + EB_PAD])
                    store_state(out_bs, EB[:, :, EB_W - EB_PAD:EB_W])
                    for g in range(KA):
                        u = next_use()
                        act.activation(Z[:, KA + g, :], ps(u), ACT.Identity,
                                       scale=vecs("pool_scale")[:, g:g + 1]).then_inc(act_read, 1)
                    w.take("dve")
                    squares(YC, SQ, KA, centered, 1)
                    root()
                    for k in range(KA):
                        act.wait_ge(xn_ready, KD + k + 1)
                        act.activation(SQ[:, k, :], YC[:, k, :], ACT.Sigmoid, scale=vecs("ln_a_g")[:, k:k + 1],
                                       bias=vecs("ln_a_b")[:, k:k + 1]).then_inc(ln_sig, 1)
                else:
                    act.wait_ge(x_ready, KD)
                    act.wait_ge(pads_made, 1)
                    act.wait_ge(c_in, 16)
                    for c in range(2 * KD):
                        u = next_use()
                        if c < KD:
                            act.copy(BG[:, c, :], ps(u)).then_inc(act_read, 1)
                        else:
                            for a, b, s in SEG:
                                ins = act.copy(EC[:, c - KD, a + EC_PAD * (1 + s):b + EC_PAD * (1 + s)], ps(u)[:, a:b])
                            ins.then_inc(act_read, 1)
                    w.take("dve", KD)
                    act.wait_ge(dve_read, w.dve.at())
                    store_state(out_cp, EC[:, :, NP_:NP_ + EC_PAD])
                    store_state(out_cs, EC[:, :, EC_W - EC_PAD:EC_W])
                w.take("dve", KD)
                squares(X, H, KD, dve_read, w.dve.at(1 - KD))
                root()
                modulate(l, 1)
                act.wait_ge(state_out, (64, 96)[l])
                for c in range(NQ):
                    u = next_use()
                    act.copy(QT[:, c, :], ps(u)).then_inc(act_read, 1)

                def tile_and_steps(t, steps):
                    before = w.use.at()
                    w.take("dve", 2)
                    act.wait_ge(shifted, t + 1)
                    flat = CAND.rearrange("p h k -> p (h k)")
                    act.activation(flat, flat, ACT.Exp).then_inc(exped, 1)
                    act.wait_ge(mm_done, before)
                    for j in range(4):
                        u = next_use()
                        act.copy(GT[:, 4 * j:4 * j + 4, :].rearrange("p a t -> p (a t)"), ps(u, 512)).then_inc(act_read, 1)
                    for j in range(2):
                        u = next_use()
                        act.copy(IT[:, j, :], ps(u, P)).then_inc(act_read, 1)
                    with loop(act, steps, *w.steps(act=8), (sub, 4), (body, 1)):
                        start = w.use.n
                        for which, s in ORDER:
                            if which == 1:
                                act.wait_ge(mm_done, w.use.at(start - w.use.n + (M2[s - 1] + 1 if s else 0)))
                                u = next_use()
                                act.copy(ROWS.rearrange("p t k -> p (t k)"), ps(u, 1024)).then_inc(act_read, 1)
                            else:
                                if s % 2 == 0:
                                    act.wait_ge(g_written[s // 2], body.at() * 16)
                                u = next_use()
                                dst = stage[:, s // 2, :, SUB * (s % 2):SUB * (s % 2) + SUB, :]
                                act.copy(dst, ps(u, 1024).rearrange("p (t g e) -> p g t e", t=SUB, e=8)).then_inc(act_read, 1)
                        sub.n += 4
                        body.n += 1

                with loop(act, 4, (w.use, 40), (w.act, 38), (w.dve, 2), (sub, 16), (body, 4)) as turn:
                    tile_and_steps(turn + 5 * l, 4)
                act.wait_ge(mm_done, w.use.at(2))
                for k in range(KD):
                    act.copy(H16[:, 0, k, :], H[:, k, :]).then_inc(h_high, 1)
                tile_and_steps(5 * l + 4, 1)

                def high(x, ahead, scale):
                    act.wait_ge(raw_in[x], group.at(1 + ahead) * 16)
                    act.wait_ge(mm_done, w.use.at())
                    act.activation(parts[x][:, 0, :], raw[x], ACT.Copy, scale=scale).then_inc(high_made[x], 1)

                act.wait_ge(mm_done, w.use.at())
                act.wait_ge(gates_ready, 5 * (l + 1))
                high("U", 0, U_SCALE)
                def expert_body(groups_ahead):
                    for grp in range(2):
                        high("V", 0, 1.0)
                        for j in range(4):
                            u = next_use()
                            act.wait_ge(w_ready, wts.at(j - 1))
                            act.activation(AG[:, j % 2, :].rearrange("p (b c) -> p b c", b=2), ps_halves(u),
                                           ACT.Gelu_apprx_tanh, scale=1.0 / U_SCALE).then_inc(act_read, 1)
                        wts.n += 4
                        if grp < groups_ahead:
                            high("U", 1, U_SCALE)
                        w.take("dve", KD)
                        group.n += 1

                with loop(act, BODIES - 1, *w.steps(act=8, dve=16), (wts, 8), (group, 2)):
                    expert_body(2)
                expert_body(1)
            squares(X, H, KD, x_ready, KD + 1)
            root()

        @block.gpsimd
        def _(pool):
            w, sub = Walk(), Count()
            steps = 0

            def link(ins):
                nonlocal steps
                steps += 1
                ins.then_inc(pool_step, 1)
                pool.wait_ge(pool_step, steps)

            pool.memset(ones[:, :], 1.0).then_inc(consts_made, 1)
            link(pool.memset(ident[:, :], 0.0))
            pool.affine_select(out=ident[:, :], in_=ident[:, :], compare_op=ALU.not_equal, fill=1.0, base=0,
                               pattern=[[-1, P]], channel_multiplier=1).then_inc(consts_made, 1)
            pool.iota(iota[:, :], [[1, P]], base=0, channel_multiplier=0,
                      allow_small_or_imprecise_dtypes=True).then_inc(consts_made, 1)
            link(pool.memset(head_mask[:, :], 1.0))
            link(pool.affine_select(out=head_mask[:, :], in_=head_mask[:, :], compare_op=ALU.is_ge, fill=0.0, base=0,
                                    pattern=[[-TOPK, HEADS]], channel_multiplier=1))
            pool.affine_select(out=head_mask[:, :], in_=head_mask[:, :], compare_op=ALU.is_ge, fill=0.0, base=TOPK - 1,
                               pattern=[[TOPK, HEADS]], channel_multiplier=-1).then_inc(consts_made, 1)
            for i in range(PB + 1):
                ins = pool.memset(inv_count[:, i:i + 1], 1.0 / (i + 1))
            link(ins)
            pool.memset(EA[:, :, 0:EA_PAD], 0.0).then_inc(consts_made, 1)
            pool.memset(EB[:, :, 0:EB_PAD], 0.0).then_inc(consts_made, 1)
            for l in range(LAYERS):
                w.take("dve", ADA_SLOTS + 1)
                if l == 0:
                    pool.wait_ge(state_in, 32)
                    pool.wait_ge(consts_made, CONSTS)
                    w.take("act", 2 * KA)
                    for g, wnd in enumerate(WINDOWS):
                        w.take("act")
                        pool.wait_ge(act_read, w.act.at())
                        src, have = EB[:, g, :], 1
                        for i in range(g + 1):
                            dst = PT[:, i % 2, :]
                            link(pool.tensor_tensor(dst[:, 2 * have - 1:EB_W], src[:, 2 * have - 1:EB_W],
                                                    src[:, have - 1:EB_W - have], ALU.add))
                            src, have = dst, 2 * have
                        for a, b, s in SEG:
                            o = EB_PAD * (1 + s)
                            link(pool.tensor_scalar(PL[:, g, a:b], src[:, a + o:b + o], 1.0 / wnd, None, ALU.mult))
                        link(pool.tensor_tensor(PL[:, g, 0:wnd], src[:, EB_PAD:EB_PAD + wnd], inv_count[:, 0:wnd], ALU.mult))
                        for a, b, s in SEG:
                            o = EB_PAD * (1 + s)
                            ins = pool.tensor_tensor(PL[:, g, a:b], PL[:, g, a:b], EB[:, g, a + o:b + o], ALU.subtract)
                        ins.then_inc(pooled, 1)
                    w.take("act", KA)
                    w.take("dve", 2)
                else:
                    pool.wait_ge(x_ready, KD)
                    pool.memset(EC[:, :, 0:EC_PAD], 0.0).then_inc(pads_made, 1)
                    pool.dma_start(EC[:, :, EC_PAD + NP_:2 * EC_PAD + NP_], state_c).then_inc(c_in, 16)
                    w.take("act", 2 * KD)
                    w.take("dve", KD)
                w.take("dve", KD + 1)
                w.take("act", NQ)

                def tile_and_steps(steps):
                    w.take("dve", 2)
                    w.take("act", 6)
                    transposed = w.act.at()
                    with loop(pool, steps, *w.steps(act=8), (sub, 4)) as turn:
                        pool.wait_ge(act_read, transposed)
                        for s in range(4):
                            tok = bass.ds(turn * STEP + SUB * s, SUB)
                            pool.wait_ge(mm_done, w.use.at(M1[s - 1] + 1 if s else -2))
                            pool.tensor_tensor(BD, GT[:, :, tok].rearrange("p a t -> p t a").unsqueeze(2)
                                               .to_broadcast([P, SUB, HEADS, TOPK]),
                                               head_mask[:, :].unsqueeze(1).unsqueeze(3).to_broadcast([P, SUB, HEADS, TOPK]),
                                               ALU.mult).then_inc(bd_ready, 1)
                        w.take("act", 8)
                        sub.n += 4

                with loop(pool, 4, (w.use, 40), (w.act, 38), (w.dve, 2), (sub, 16)):
                    tile_and_steps(4)
                tile_and_steps(1)
                for s in range(2):
                    pool.wait_ge(g_written[s], 16 * ((l + 1) * STEPS + 1))
                pool.memset(ACCF[:, :], 0.0).then_inc(acc_zero, 1)
                w.take("act", 8 * BODIES)
                w.take("dve", 16 * BODIES)

        @block.vector
        def _(dve):
            w, step, sub, group, wf = Walk(), Count(), Count(), Count(), Count()
            carried = [0]

            def next_use():
                dve.wait_ge(mm_done, w.use.at(1))
                return w.take("dve")

            def link(ins):
                ins.then_inc(dve_step, 1)
                step.n += 1
                settle(dve_step, step.at())

            def settle(semaphore, value):
                dve.wait_ge(semaphore, value)
                if not isinstance(value, int):
                    carried[0] += 1
                    dve.memset(carrier[:, carried[0] % 3:carried[0] % 3 + 1], 0.0)

            def inverse_root(n, width):
                u = next_use()
                dve.tensor_scalar(stat[:, 0, :], ps(u), 1.0 / width, EPS, ALU.mult, ALU.add).then_inc(dve_read, 1)
                dve.wait_ge(std_ready, n)
                link(dve.reciprocal(stat[:, 2, :], stat[:, 1, :]))
                link(dve.tensor_tensor(stat[:, 1, :], stat[:, 0, :], stat[:, 2, :], ALU.mult))
                link(dve.tensor_tensor(stat[:, 1, :], stat[:, 1, :], stat[:, 2, :], ALU.mult))
                link(dve.tensor_scalar(stat[:, 1, :], stat[:, 1, :], -0.5, 1.5, ALU.mult, ALU.add))
                link(dve.tensor_tensor(stat[:, 2, :], stat[:, 1, :], stat[:, 2, :], ALU.mult))

            def norm_x(n):
                inverse_root(n, D)
                for k in range(KD):
                    dve.tensor_tensor(H[:, k, :], X[:, k, :], stat[:, 2, :], ALU.mult).then_inc(xn_ready, 1)

            def residual(l, gate, experts):
                for k in range(KD):
                    u = None if experts else next_use()
                    for a, b, s in SEG:
                        y = ACC[:, k, a:b] if experts else ps(u)[:, a:b]
                        ins = dve.scalar_tensor_tensor(out=X[:, k, a:b], in0=y, scalar=mod[:, l, mod_at[gate] * KD + k, s:s + 1],
                                                       in1=X[:, k, a:b], op0=ALU.mult, op1=ALU.add)
                    ins.then_inc(x_ready if experts else dve_read, 1)
                dve.wait_ge(x_ready if experts else dve_read, KD * (l + 1) if experts else w.dve.at())

            for i in range(2):
                dve.memset(carrier[:, i:i + 1], 0.0).then_inc(w_ready, 1)
            dve.wait_ge(vec_in, 16)
            dve.wait_ge(c_sigmoid, 1)
            flat = cact[:, :, :].rearrange("p k s -> p (k s)")
            dve.tensor_tensor(flat, flat, vecs("c"), ALU.mult).then_inc(cact_ready, 1)
            dve.wait_ge(consts_made, CONSTS)
            dve.wait_ge(x_in, 16)
            for l in range(LAYERS):
                bias = vecs("b_ada")[:, l * 6 * KD:(l + 1) * 6 * KD]
                with loop(dve, ADA_SLOTS // 4, *w.steps(dve=4)) as turn:
                    for s in range(4):
                        u = next_use()
                        at = turn * 16 + 4 * s
                        dve.tensor_tensor(mod[:, l, bass.ds(at, 4), :], ps(u, 8).rearrange("p (m s) -> p m s", s=2),
                                          bias[:, bass.ds(at, 4)].unsqueeze(2).to_broadcast([P, 4, 2]),
                                          ALU.add).then_inc(dve_read, 1)
                dve.wait_ge(dve_read, w.dve.at())
                for which, (sc, g) in enumerate((("sc1", "norm_mix_g"), ("sc2", "norm_ffn_g"))):
                    at = mod_at[sc] * KD
                    gv = vecs(g)[:, l * KD:(l + 1) * KD].unsqueeze(2).to_broadcast([P, KD, 2])
                    link(dve.tensor_scalar(scale[:, l, which, :, :], mod[:, l, at:at + KD, :], 1.0, None, ALU.add))
                    ins = dve.tensor_tensor(scale[:, l, which, :, :], scale[:, l, which, :, :], gv, ALU.mult)
                at = mod_at["g2"] * KD
                link(ins)
                dve.tensor_scalar(mod[:, l, at:at + KD, :], mod[:, l, at:at + KD, :], 1.0 / W_SCALE, None,
                                  ALU.mult).then_inc(mod_ready, 1)
                norm_x((1, 4)[l])
                if l == 0:
                    dve.wait_ge(state_in, 32)
                    w.take("act", KA)
                    for c in range(KA):
                        w.take("act")
                        dve.wait_ge(act_read, w.act.at())
                        for a, b, s in SEG:
                            o = EA_PAD * (1 + s)
                            ins = dve.tensor_tensor(EA[:, c, a + o:b + o], EA[:, c, a + o:b + o], SG[:, c % 2, a:b], ALU.mult)
                        ins.then_inc(glu_ready, 1)
                    w.take("act", 2 * KA)
                    dve.wait_ge(glu_ready, KA)
                    wide = T + EA_PAD
                    for i in range(WA):
                        for c in range(KA):
                            tap = vecs("dw_a")[:, c * WA + i:c * WA + i + 1]
                            if i == 0:
                                ins = dve.tensor_scalar(CONV[:, c, :], EA[:, c, 0:wide], tap, vecs("db_a")[:, c:c + 1],
                                                        ALU.mult, ALU.add)
                            else:
                                dve.wait_ge(dve_step, step.n - (KA - 1 if i < WA - 1 else KA - 1 - c))
                                ins = dve.scalar_tensor_tensor(out=CONV[:, c, :], in0=EA[:, c, i:i + wide], scalar=tap,
                                                               in1=CONV[:, c, :], op0=ALU.mult, op1=ALU.add)
                            if i < WA - 1:
                                ins.then_inc(dve_step, 1)
                                step.n += 1
                            else:
                                ins.then_inc(conv_ready, 1)
                    dve.wait_ge(conv_ready, KA)
                    u = next_use()
                    for k in range(KA):
                        for a, b, s in SEG:
                            ins = dve.scalar_tensor_tensor(out=YC[:, k, a:b], in0=ps(u)[:, a:b], scalar=-1.0 / DA,
                                                           in1=CONV[:, k, a + s * EA_PAD:b + s * EA_PAD],
                                                           op0=ALU.mult, op1=ALU.add)
                        ins.then_inc(centered, 1)
                    dve.wait_ge(centered, KA)
                    dve.tensor_copy(carrier[:, 3:4], ps(u, 1)).then_inc(dve_read, 1)
                    inverse_root(2, DA)
                    for k in range(KA):
                        dve.tensor_tensor(YC[:, k, :], YC[:, k, :], stat[:, 2, :], ALU.mult).then_inc(xn_ready, 1)
                    for k in range(KA):
                        dve.wait_ge(ln_sig, k + 1)
                        link(dve.tensor_scalar(YC[:, k, :], YC[:, k, :], vecs("ln_a_g")[:, k:k + 1],
                                               vecs("ln_a_b")[:, k:k + 1], ALU.mult, ALU.add))
                        dve.tensor_tensor(Z[:, k, :], YC[:, k, :], SQ[:, k, :], ALU.mult).then_inc(z_ready, 1)
                else:
                    w.take("act", KD)
                    wide = T + EC_PAD
                    first = w.act.n
                    w.take("act", KD)
                    for c in range(KD):
                        dve.wait_ge(act_read, first + c + 1)
                        u = next_use()
                        for a, b, s in SEG:
                            o = EC_PAD * (1 + s)
                            ins = dve.tensor_tensor(EC[:, c, a + o:b + o], ps(u)[:, a:b], EC[:, c, a + o:b + o], ALU.mult)
                        ins.then_inc(dve_read, 1)
                        dve.wait_ge(dve_read, w.dve.at())
                        dve.wait_ge(pads_made, 1)
                        dve.wait_ge(c_in, 16)
                        for i in range(WC):
                            tap = vecs("dw_c")[:, c * WC + i:c * WC + i + 1]
                            if i == 0:
                                link(dve.tensor_scalar(YO[:, c, 0:wide], EC[:, c, 0:wide], tap, None, ALU.mult))
                            else:
                                link(dve.scalar_tensor_tensor(out=YO[:, c, 0:wide], in0=EC[:, c, i:i + wide], scalar=tap,
                                                              in1=YO[:, c, 0:wide], op0=ALU.mult, op1=ALU.add))
                        for a, b, s in SEG:
                            o = EC_PAD * s
                            ins = dve.tensor_tensor(Z[:, c, a:b], YO[:, c, a + o:b + o], BG[:, c, a:b], ALU.mult)
                        ins.then_inc(z_ready, 1)
                residual(l, "g1", False)
                norm_x((3, 5)[l])
                w.take("act", NQ)

                def tile_and_steps(t, steps):
                    settle(mm_done, w.use.at())
                    uu = [next_use(), next_use()]
                    settle(mm_done, w.use.at())

                    def score(q):
                        return PS[:, uu[q // 8] % PAIRS, (q % 8) * P:(q % 8 + 1) * P]

                    def best(q, lo):
                        return V16[:, q // 2, q % 2, lo:lo + 8]

                    for q in range(NQ):
                        ins = dve.max(best(q, 0), score(q))
                    link(ins)
                    for q in range(NQ):
                        dve.max_index(I16[:, q // 2, q % 2, 0:8], best(q, 0), score(q))
                        ins = dve.match_replace(ZT[:, q, :], best(q, 0), score(q), NEG)
                        if q % 8 == 7:
                            ins.then_inc(dve_read, 1)
                    settle(dve_read, w.dve.at())
                    for q in range(NQ):
                        ins = dve.max(best(q, 8), ZT[:, q, :])
                    link(ins)
                    for q in range(NQ):
                        ins = dve.max_index(I16[:, q // 2, q % 2, 8:16], best(q, 8), ZT[:, q, :])
                    link(ins)
                    shape = [P, HEADS, TOPK, TOPK]
                    link(dve.tensor_tensor(CAND.rearrange("p h (a b) -> p h a b", a=TOPK),
                                           V16[:, :, 0, :].unsqueeze(3).to_broadcast(shape),
                                           V16[:, :, 1, :].unsqueeze(2).to_broadcast(shape), ALU.add))
                    for h in range(HEADS):
                        ins = dve.max(C8[:, h, 0:8], CAND[:, h, :])
                    link(ins)
                    for h in range(HEADS):
                        ins = dve.match_replace(ZAP[:, h, :], C8[:, h, 0:8], CAND[:, h, :], NEG)
                    link(ins)
                    dve.tensor_tensor(CAND, CAND, C8[:, :, 0:1].to_broadcast([P, HEADS, TOPK * TOPK]),
                                      ALU.subtract).then_inc(shifted, 1)
                    for h in range(HEADS):
                        ins = dve.max(C8[:, h, 8:16], ZAP[:, h, :])
                    link(ins)
                    dve.tensor_copy(IF.rearrange("p j h k -> p h j k"), I16)
                    for h in range(HEADS):
                        ins = dve.match_replace(ZAP[:, h, :], C8[:, h, 8:16], ZAP[:, h, :], NEG)
                    link(ins)
                    dve.wait_ge(exped, t + 1)
                    link(dve.scalar_tensor_tensor(out=ZAP, in0=ZAP, scalar=NEG, in1=CAND, op0=ALU.is_equal, op1=ALU.mult))
                    link(dve.tensor_reduce(ZS, ZAP, AX.X, ALU.add))
                    link(dve.reciprocal(RZ, ZS))
                    for h in range(HEADS):
                        ins = dve.tensor_scalar(GG[:, :, h * TOPK:(h + 1) * TOPK], ZAP[:, h, :].rearrange("p (a b) -> p a b", a=TOPK),
                                                RZ[:, h:h + 1], None, ALU.mult)
                    ins.then_inc(gates_ready, 1)
                    w.take("act", 6)
                    transposed = w.act.at()
                    with loop(dve, steps, *w.steps(act=8), (sub, 4)) as turn:
                        dve.wait_ge(act_read, transposed)
                        for s in range(4):
                            tok = bass.ds(turn * STEP + SUB * s, SUB)
                            dve.wait_ge(mm_done, w.use.at(M1[s - 1] + 1 if s else -2))
                            dve.tensor_tensor(O2[:, :, :], iota[:, :].unsqueeze(1).to_broadcast([P, SUB, P]),
                                              IT[:, 1, tok].unsqueeze(2).to_broadcast([P, SUB, P]),
                                              ALU.is_equal).then_inc(o2_ready, 1)
                            dve.wait_ge(mm_done, w.use.at((-1, 0, 3, 5)[s]))
                            dve.tensor_tensor(O1[:, s % 2, :, :], iota[:, :].unsqueeze(1).to_broadcast([P, SUB, P]),
                                              IT[:, 0, tok].unsqueeze(2).to_broadcast([P, SUB, P]),
                                              ALU.is_equal).then_inc(o1_ready, 1)
                        w.take("act", 8)
                        sub.n += 4

                with loop(dve, 4, (w.use, 40), (w.act, 38), (w.dve, 2), (sub, 16), (step, TILE_LINKS)) as turn:
                    tile_and_steps(turn + 5 * l, 4)
                tile_and_steps(5 * l + 4, 1)

                for k in range(KD):
                    dve.wait_ge(h_high, l * KD + k + 1)
                    dve.tensor_tensor(H16[:, 1, k, :], H[:, k, :], H16[:, 0, k, :], ALU.subtract).then_inc(h_split, 1)
                dve.wait_ge(acc_zero, l + 1)

                def low(x, ahead, scale):
                    dve.wait_ge(high_made[x], group.at(1 + ahead))
                    dve.scalar_tensor_tensor(out=parts[x][:, 1, :], in0=raw[x], scalar=scale, in1=parts[x][:, 0, :],
                                             op0=ALU.mult, op1=ALU.subtract).then_inc(split[x], 1)

                low("U", 0, U_SCALE)

                def expert_body(turn, groups_ahead):
                    dve.wait_ge(g_in, turn * 16 + 16 * (l * BODIES + 1))
                    g = (GB[:, bass.ds((turn % 2) * (T * 8), T * 8)] if not isinstance(turn, int) else
                         GB[:, (turn % 2) * (T * 8):(turn % 2 + 1) * (T * 8)]).rearrange("p (t e) -> p t e", e=8)
                    for grp in range(2):
                        low("V", 0, 1.0)
                        dve.wait_ge(mm_done, w.use.at(-12))
                        for j in range(4):
                            w.take("act")
                            dve.wait_ge(act_read, w.act.at())
                            wf.n += 1
                            ag = AG[:, j % 2, :]
                            dve.tensor_tensor(ag, ag, g[:, :, 4 * grp + j], ALU.mult).then_inc(wf_ready, 1)
                            dve.wait_ge(wf_ready, wf.at())
                            dve.tensor_scalar(WT[:, grp, 0, j, :], ag, W_SCALE, None, ALU.mult).then_inc(w_high, 1)
                            dve.wait_ge(w_high, wf.at())
                            dve.scalar_tensor_tensor(out=WT[:, grp, 1, j, :], in0=ag, scalar=W_SCALE, in1=WT[:, grp, 0, j, :],
                                                     op0=ALU.mult, op1=ALU.subtract).then_inc(w_ready, 1)
                        if grp < groups_ahead:
                            low("U", 1, U_SCALE)
                        group.n += 1
                        for c in range(KD):
                            dve.wait_ge(dve_read, w.dve.at(1 - KD))
                            u = next_use()
                            acc = ACC[:, c, :].rearrange("p (b c) -> p b c", b=2)
                            dve.tensor_tensor(acc, ps_halves(u), acc, ALU.add).then_inc(dve_read, 1)

                with loop(dve, BODIES - 1, *w.steps(act=8, dve=16), (wf, 8), (group, 2)) as turn:
                    expert_body(turn, 2)
                expert_body(BODIES - 1, 1)
                dve.wait_ge(dve_read, w.dve.at())
                residual(l, "g2", True)
            inverse_root(6, D)
            for k in range(KD):
                dve.scalar_tensor_tensor(out=H[:, k, :], in0=X[:, k, :], scalar=vecs("final_g")[:, k:k + 1],
                                         in1=stat[:, 2, :], op0=ALU.mult, op1=ALU.mult).then_inc(y_ready, 1)


def kernel(**inputs):
    import concourse.bacc as _bacc
    from concourse.bass_utils import run_bass_kernel_spmd as _run

    x = {k: np.asarray(v) for k, v in inputs.items()}

    def chunks(a):
        n, f = a.shape
        return np.ascontiguousarray(a.T.reshape(f // P, P, n).transpose(1, 0, 2))

    def slots(wt):
        k, m = wt.shape
        return wt.reshape(k // P, P, m // 512, 512).transpose(2, 1, 0, 3).reshape(m // 512, P, SLOT)

    def u_slots(u):
        return u.reshape(GROUPS, 512, KD, P).transpose(0, 3, 2, 1).reshape(GROUPS, P, SLOT)

    def v_slots(v):
        return v.reshape(GROUPS, 4, P, D).transpose(0, 2, 1, 3).reshape(GROUPS, P, SLOT)

    cols = {
        "norm_mix_g": x["norm_mix_g"].reshape(-1, P).T,
        "norm_ffn_g": x["norm_ffn_g"].reshape(-1, P).T,
        "b_ada": x["b_ada"].reshape(-1, P).T,
        "db_a": x["db_a"].reshape(-1, P).T,
        "ln_a_g": x["ln_a_g"].reshape(-1, P).T,
        "ln_a_b": x["ln_a_b"].reshape(-1, P).T,
        "pool_scale": x["pool_scale"].reshape(-1, P).T,
        "final_g": x["final_g"].reshape(-1, P).T,
        "dw_a": chunks(x["dw_a"][0]).reshape(P, -1),
        "dw_c": chunks(x["dw_c"][0]).reshape(P, -1),
        "c": chunks(np.concatenate([x["c_prompt"], x["c_sample"]])).reshape(P, -1),
    }
    front = []
    for l in range(LAYERS):
        front += [slots(x["w_ada"][l]), slots((x["w_in_even"], x["w_in_odd"])[l][0]),
                  slots((x["w_out_even"], x["w_out_odd"])[l][0]), slots(x["peer_wq"][l])]
    keys = np.stack([x["peer_k1"], x["peer_k2"]], axis=2)
    arrays = {
        "xT": chunks(np.concatenate([x["x_prompt"][0], x["x_sample"][0]])),
        "vectors": np.concatenate([cols[name] for name, _ in VECTORS], axis=1),
        "state_a": chunks(x["state_conv_a"][0, 0]),
        "state_b": chunks(x["state_pool_b"][0, 0]),
        "state_c": chunks(x["state_conv_c"][0, 0]),
        "w_pool": x["w_pool"][0].transpose(1, 0, 2),
        "keys": keys.reshape(LAYERS, NQ, NKEYS, P).transpose(0, 3, 1, 2),
        "front_w": np.concatenate(front),
        "U": np.stack([u_slots(u) for u in x["peer_u"]]),
        "V": np.stack([v_slots(v) for v in x["peer_v"]]),
    }
    arrays = {k: np.ascontiguousarray(v) for k, v in arrays.items()}
    outs = {"y": (P, KD, T), "new_ap": (P, KA, EA_PAD), "new_as": (P, KA, EA_PAD), "new_bp": (P, KA, EB_PAD),
            "new_bs": (P, KA, EB_PAD), "new_cp": (P, KD, EC_PAD), "new_cs": (P, KD, EC_PAD)}
    nc = _bacc.Bacc("TRN2", target_bir_lowering=False, num_devices=1)
    args = [nc.dram_tensor(k, v.shape, F32, kind="ExternalInput").ap() for k, v in arrays.items()]
    args += [nc.dram_tensor(k, shape, F32, kind="ExternalOutput").ap() for k, shape in outs.items()]
    args.append(nc.dram_tensor("gates_dram", (P, BODIES, T, 8), F32, kind="Internal").ap())
    build(nc, *args)
    r = _run(nc, [arrays], core_ids=[0]).results[0]

    def rows(a):
        a = np.asarray(a)
        return np.ascontiguousarray(a.transpose(2, 1, 0).reshape(a.shape[2], -1))

    y = rows(r["y"])
    new = [rows(r[k])[None, None] for k in ("new_ap", "new_bp", "new_cp", "new_as", "new_bs", "new_cs")]
    return (y[None, :NP_], y[None, NP_:], *new)
```

```python
from contextlib import ExitStack, contextmanager

import numpy as np

import concourse.bass as bass
from concourse import mybir

ALU = mybir.AluOpType
ACT = mybir.ActivationFunctionType
AX = mybir.AxisListType
F32 = mybir.dt.float32
F16 = mybir.dt.float16
U32 = mybir.dt.uint32

P = 128
D = 1024
KD = D // P
LAYERS = 2
NP_, NS_ = 512, 32
T = NP_ + NS_
HALF = T // 2
DA = 512
KA = DA // P
WA, WC = 31, 3
WINDOWS = (2, 4, 8, 16)
PB = max(WINDOWS) - 1
HEADS, NKEYS, TOPK = 8, 128, 16
NQ = 2 * HEADS
EPS = 1e-6
NEG = float(np.float32(-3.0e38))

SLOT = 4096
RING = 4
PAIRS = 4
U_SCALE, W_SCALE = 32.0, 16.0
GROUPS = NKEYS // 4
BODIES = GROUPS // 2
AHEAD = 10
TILES = 5
SUB = 8
STEP = 32
ADA_SLOTS, IN_SLOTS, OUT_SLOTS, Q_SLOTS = 12, (3, 6), 2, 4
FRONT = tuple(IN_SLOTS[l] + OUT_SLOTS + Q_SLOTS + (ADA_SLOTS * LAYERS if l == 0 else 0) for l in range(LAYERS))
ORDER = ((1, 0), (1, 1), (2, 0), (1, 2), (2, 1), (1, 3), (2, 2), (2, 3))
M1 = (0, 1, 3, 5)

EA_PAD, EB_PAD, EC_PAD = WA - 1, PB, WC - 1
EA_W, EB_W, EC_W = T + 2 * EA_PAD, T + 2 * EB_PAD, T + 2 * EC_PAD

VECTORS = [("norm_mix_g", LAYERS * KD), ("norm_ffn_g", LAYERS * KD), ("b_ada", LAYERS * 6 * KD), ("db_a", KA),
           ("ln_a_g", KA), ("ln_a_b", KA), ("pool_scale", KA), ("final_g", KD), ("dw_a", KA * WA),
           ("dw_c", KD * WC), ("c", KD * 2)]
VEC_AT = {}
VEC_N = 0
for _name, _n in VECTORS:
    VEC_AT[_name] = (VEC_N, _n)
    VEC_N += _n


class Count:

    def __init__(self, n=0):
        self.n, self.turns = n, []

    def at(self, ahead=0):
        value = self.n + ahead
        for turn, per in self.turns:
            value = turn * per + value
        return value

    def over(self, by):
        value = self.n // by
        for turn, per in self.turns:
            value = turn * (per // by) + value
        return value


@contextmanager
def loop(eng, times, *steps):
    with eng.Fori(0, times) as turn:
        starts = [c.n for c, _ in steps]
        for c, per in steps:
            c.turns.append((turn, per))
        yield turn
        for (c, per), start in zip(steps, starts):
            c.turns.pop()
            assert c.n - start == per, (c.n - start, per)
            c.n = start + per * times


class Walk:

    def __init__(self):
        self.use, self.act, self.dve = Count(), Count(), Count()

    def take(self, reader, n=1):
        self.use.n += n
        (self.act if reader == "act" else self.dve).n += n
        return self.use.n - 1

    def steps(self, act=0, dve=0):
        return (self.use, act + dve), (self.act, act), (self.dve, dve)


def _schedule():
    use = act = 0
    last, residual, gate_act, expert_use, expert_act, expert_end = [], [], [], [], [], []
    ada = [8 * (s // 4) + M1[s % 4] + 1 for s in range(ADA_SLOTS)]
    for l in range(LAYERS):
        if l == 0:
            last += ada
            use += 2 * ADA_SLOTS
            act += 2 * ADA_SLOTS
        use += 1
        last += [use + 4 * (s + 1) for s in range(IN_SLOTS[l])]
        use += 4 * IN_SLOTS[l]
        act += (12, 16)[l]
        if l == 0:
            last += [use + KA + n for n in ada]
            use += KA + 2 * ADA_SLOTS + 2
            act += KA + 2 * ADA_SLOTS
        last += [use + 4 * (s + 1) for s in range(OUT_SLOTS)]
        use += 4 * OUT_SLOTS
        residual.append(use - act)
        use += 1
        last += [use + 4 * (s + 1) for s in range(Q_SLOTS)]
        use += NQ
        act += NQ
        gate_act.append(act)
        use += TILES * 12 + (T // STEP) * 4
        act += TILES * 10 + (T // STEP) * 4
        expert_use.append(use)
        expert_act.append(act)
        use += 8 * AHEAD + 12 * (GROUPS - AHEAD)
        act += 4 * (GROUPS - AHEAD)
        expert_end.append(use)
    return last, residual, gate_act, expert_use, expert_act, expert_end


LAST_USE, RESIDUAL, GATE_ACT, EXPERT_USE, EXPERT_ACT, EXPERT_END = _schedule()
TILE_LINKS = 17


def build(nc, xT, vectors, state_a, state_b, state_c, w_pool, keys, front_w, U, V,
          out_y, out_ap, out_as, out_bp, out_bs, out_cp, out_cs, gates_dram, act_dram, x_dram):
    with ExitStack() as ctx:
        def sb(name, shape, dt=F32):
            return ctx.enter_context(nc.sbuf_tensor(name, shape, dt))

        def sem(name):
            return ctx.enter_context(nc.semaphore(name))

        X = sb("X", [P, KD, T])
        H = sb("H", [P, KD, T])
        ACCF = sb("ACC", [P, KD * T])
        ACC = ACCF[:, :].rearrange("p (k t) -> p k t", k=KD)
        Z = ACC
        ring = sb("ring", [P, RING, SLOT])
        keyT = sb("keyT", [P, NQ, NKEYS])
        vec = sb("vec", [P, VEC_N])
        wpool = sb("wpool", [P, KA, P])
        ones = sb("ones", [P, P])
        ident = sb("ident", [P, P])
        iota = sb("iota", [P, P])
        inv_count = sb("inv_count", [P, PB + 1])
        mod = sb("mod", [P, LAYERS, 6 * KD, 2])
        scale = sb("scale", [P, LAYERS, 2, KD, 2])
        cact = sb("cact", [P, KD, 2])
        stat = sb("stat", [P, 3, T])
        carrier = sb("carrier", [P, 4])
        arena = sb("arena", [P, 18176])

        def part(at, *shape, dt=F32):
            n = int(np.prod(shape))
            assert at + n <= 18176, at + n
            v = arena[:, at:at + n]
            if dt is not F32:
                v = v.bitcast(dt)
            names = "abcd"[:len(shape)]
            if len(shape) > 1:
                sizes = {k: s for k, s in zip(names, shape)}
                v = v.rearrange(f"p ({' '.join(names)}) -> p {' '.join(names)}", **sizes)
            return v

        def vecs(name):
            at, n = VEC_AT[name]
            return vec[:, at:at + n]

        mod_rows = stat[:, :, :].rearrange("p a t -> p (a t)")[0:2, 0:1024].rearrange("c (b n) -> c b n", b=2)
        EA = part(0, KA, EA_W)
        EB = part(2416, KA, EB_W)
        CONV = part(4712, KA, EB_W)
        YC = part(7008, KA, T)
        SQ = part(9184, KA, T)
        PL = part(11360, KA, T)
        SG = part(13536, 2, T)
        PT = part(14624, 2, EB_W)
        BG = part(0, KD, T)
        EC = part(4352, KD, EC_W)
        YO = part(8736, KD, EC_W)
        QT = part(0, NQ, T)
        CAND = part(8704, HEADS, TOPK * TOPK)
        ZAP = part(10752, HEADS, TOPK * TOPK)
        ZT = part(10752, NQ, NKEYS)
        PICK = part(8704, P, TOPK)
        PLACE = part(10752, 2, P, dt=U32)
        PLF = part(11008, 2, P)
        IT = part(12800, 2, P)
        GT = part(13056, P)
        O1 = part(13184, 2, SUB, P)
        O2 = part(15232, 2, SUB, P)
        small = stat[:, :, :].rearrange("p a t -> p (a t)")
        V16 = small[:, 0:256].rearrange("p (h j k) -> p h j k", h=HEADS, j=2)
        I16 = small[:, 256:512].bitcast(U32).rearrange("p (h j k) -> p h j k", h=HEADS, j=2)
        IF = small[:, 512:768].rearrange("p (h j k) -> p h j k", h=HEADS, j=2)
        C8 = small[:, 768:896].rearrange("p (h k) -> p h k", h=HEADS)
        ZS = small[:, 896:904]
        RZ = small[:, 904:912]
        GG = small[:, 912:1040].rearrange("p (h k) -> p h k", h=HEADS)
        P8 = small[:, 1040:1168].bitcast(U32).rearrange("p (h k) -> p h k", h=HEADS)
        KEYS = small[:, 1168:1424].rearrange("p (j n) -> p j n", j=2)
        stage = ACCF[:, 0:4096].rearrange("p (s g t e) -> p s g t e", s=2, g=BODIES, t=16)
        H16 = X[:, :, :].rearrange("p k t -> p (k t)").bitcast(F16).rearrange("p (s k t) -> p s k t", s=2, k=KD)
        ahead = H[:, :, :].rearrange("p (a j) t -> p a j t", a=2)
        AB = part(0, 2, 4, T)
        GB = arena[:, 4352:4352 + 2 * T * 8]
        WT = part(13056, 2 * 4 * T).bitcast(F16).rearrange("p (g s j t) -> p g s j t", g=2, s=2, j=4)
        AG = stat[:, 0:2, :]
        raw = [ring[:, i, :] for i in range(2)]
        parts = [ring[:, 2 + i, :].bitcast(F16).rearrange("p (s n) -> p s n", s=2) for i in range(2)]

        PS = ctx.enter_context(nc.psum_tensor("PS", [P, PAIRS, 1024], F32))

        vec_in, x_in, state_in, pool_in, keys_in = (sem(x) for x in "vec_in x_in state_in pool_in keys_in".split())
        slot_in = [sem(f"slot_in{i}") for i in range(RING)]
        mm_done = sem("mm_done")
        act_read = sem("act_read")
        dve_read = sem("dve_read")
        consts_made, pads_made, c_in = sem("consts_made"), sem("pads_made"), sem("c_in")
        c_sigmoid, cact_ready, mod_ready = sem("c_sigmoid"), sem("cact_ready"), sem("mod_ready")
        x_ready, sq_ready, std_ready, xn_ready, h_ready = (sem(x) for x in "x_ready sq_ready std_ready xn_ready h_ready".split())
        glu_ready, pooled, conv_ready, centered, ln_sig, z_ready = (
            sem(x) for x in "glu_ready pooled conv_ready centered ln_sig z_ready".split())
        shifted, exped, gates_ready = sem("shifted"), sem("exped"), sem("gates_ready")
        o1_ready, o2_ready, weighted, keys_found = (sem(x) for x in "o1_ready o2_ready weighted keys_found".split())
        g_written = [sem(f"g_written{i}") for i in range(2)]
        raw_in = [sem(f"raw_in{i}") for i in range(2)]
        high_made = [sem(f"high_made{i}") for i in range(2)]
        split = [sem(f"split{i}") for i in range(2)]
        act_stored = [sem(f"act_stored{i}") for i in range(2)]
        act_in = [sem(f"act_in{i}") for i in range(2)]
        x_stored, x_back = sem("x_stored"), sem("x_back")
        h_high, h_split, wf_ready, w_high = sem("h_high"), sem("h_split"), sem("wf_ready"), sem("w_high")
        g_in, w_ready, acc_zero = sem("g_in"), sem("w_ready"), sem("acc_zero")
        dve_step, pool_step, y_ready, y_out, state_out = (sem(x) for x in "dve_step pool_step y_ready y_out state_out".split())

        SEG = ((0, NP_, 0), (NP_, T, 1))
        mod_at = {"sh1": 0, "sc1": 1, "g1": 2, "sh2": 3, "sc2": 4, "g2": 5}
        CONSTS = 5
        NORM = (0, KD + KA, 2 * KD + KA, 3 * KD + KA, 4 * KD + KA)
        STEPS = T // STEP
        PASSES = ((0, 0), (0, 1), (1, 0))

        def ps(u, n=T):
            return PS[:, u % PAIRS, 0:n]

        def ps_halves(u):
            return PS[:, u % PAIRS, :].rearrange("p (b c) -> p b c", b=2)[:, :, 0:HALF]

        block = ctx.enter_context(nc.Block())

        @block.sync
        def _(sp):
            def load(f):
                if f == FRONT[0] + (-FRONT[0]) % RING or f == FRONT[0] + (1 - FRONT[0]) % RING:
                    sp.wait_ge(split[f % RING], GROUPS)
                elif FRONT[0] <= f < FRONT[0] + RING:
                    sp.wait_ge(mm_done, EXPERT_END[0])
                elif f >= RING:
                    sp.wait_ge(mm_done, LAST_USE[f - RING])
                sp.dma_start(ring[:, f % RING, :], front_w[f]).then_inc(slot_in[f % RING], 16)

            def load_raw(lane, source, l, group, n):
                if n is not None:
                    sp.wait_ge(split[lane], n)
                src = source[l, group] if isinstance(group, int) else \
                    source[l, bass.ds(group, 1)].rearrange("o p n -> (o p) n")
                sp.dma_start(raw[lane], src).then_inc(raw_in[lane], 16)

            sp.dma_start(vec[:, :], vectors).then_inc(vec_in, 16)
            sp.dma_start(X[:, :, :], xT).then_inc(x_in, 16)
            f = 0
            view = gates_dram.rearrange("p g t e -> g p (t e)")
            for s in range(2):
                sp.sem_inc(g_written[s], 16)
                sp.sem_inc(act_stored[s], 16)
            for l in range(LAYERS):
                while f < sum(FRONT[:l + 1]):
                    load(f)
                    f += 1
                    if f == sum(FRONT[:l]) + 2 * RING:
                        sp.dma_start(keyT[:, :, :], keys[l]).then_inc(keys_in, 16)
                sp.wait_ge(dve_read, RESIDUAL[l])
                sp.dma_start(x_dram, X[:, :, :].rearrange("p k t -> p (k t)")).then_inc(x_stored, 16)
                for lane in range(2):
                    sp.wait_ge(mm_done, LAST_USE[max(k for k in range(f) if k % RING == lane)])
                    load_raw(lane, U, l, lane, None)

                def gate_tile(tile, n_steps):
                    last_tile = isinstance(tile, int)
                    for lane in range(2):
                        load_raw(lane, V if last_tile else U, l, lane if last_tile else tile * 2 + (2 + lane),
                                 tile + (l * GROUPS + 1))
                    for lane in range(2):
                        sp.wait_ge(act_read, tile * 26 + (GATE_ACT[l] + 4 * lane + 4))
                        at = tile * 2 + lane
                        dst = act_dram[:, at, :] if last_tile else act_dram[:, bass.ds(at, 1), :].rearrange("p o n -> p (o n)")
                        sp.dma_start(dst, ahead[:, lane, :, :].rearrange("p j t -> p (j t)")).then_inc(act_stored[lane], 16)
                    if last_tile:
                        spill(tile, 0)
                    else:
                        with sp.Fori(0, n_steps) as step:
                            spill(tile, step)

                def spill(tile, step):
                    for s in range(2):
                        sp.wait_ge(act_read, tile * 26 + step * 4 + (GATE_ACT[l] + 10 + 2 * s + 2))
                        sp.dma_start(gates_dram[:, :, bass.ds(tile * P + step * STEP + 16 * s, 16), :],
                                     stage[:, s, :, :, :]).then_inc(g_written[s], 16)

                with sp.Fori(0, TILES - 1) as tile:
                    gate_tile(tile, P // STEP)
                gate_tile(TILES - 1, 1)
                for s in range(2):
                    sp.wait_ge(g_written[s], 16 * ((l + 1) * STEPS + 1))
                    sp.wait_ge(act_stored[s], 16 * ((l + 1) * TILES + 1))
                sp.wait_ge(mm_done, EXPERT_USE[l])
                sp.wait_ge(act_read, EXPERT_ACT[l])
                for k in range(2):
                    if k:
                        sp.wait_ge(g_in, 16 * (l * BODIES + k))
                    sp.dma_start(GB[:, k * T * 8:(k + 1) * T * 8], view[k]).then_inc(g_in, 16)
                    sp.dma_start(AB[:, k, :, :].rearrange("p j t -> p (j t)"), act_dram[:, k, :]).then_inc(act_in[k], 16)

                def next_g(body, static=False):
                    sp.wait_ge(w_ready, body * 8 + (l * NKEYS + 10))
                    sp.wait_ge(g_in, body * 16 + 16 * (l * BODIES + 2))
                    if isinstance(body, int):
                        dst, src = GB[:, (body % 2) * T * 8:(body % 2 + 1) * T * 8], view[body + 2]
                    else:
                        dst = GB[:, bass.ds((body % 2) * (T * 8), T * 8)]
                        src = view[bass.ds(body + 2, 1)].rearrange("o p n -> (o p) n")
                    sp.dma_start(dst, src).then_inc(g_in, 16)

                with sp.Fori(0, AHEAD // 2 - 1) as body:
                    for lane in range(2):
                        group = body * 2 + (2 + lane)
                        load_raw(lane, V, l, group, body + (l * GROUPS + TILES + 1))
                        sp.wait_ge(w_ready, body * 8 + (l * NKEYS + 4 * lane + 4 + 2))
                        sp.dma_start(AB[:, lane, :, :].rearrange("p j t -> p (j t)"),
                                     act_dram[:, bass.ds(group, 1), :].rearrange("p o n -> p (o n)")).then_inc(act_in[lane], 16)
                    next_g(body)
                for lane in range(2):
                    load_raw(lane, (U, V)[lane], l, AHEAD, l * GROUPS + AHEAD)
                next_g(AHEAD // 2 - 1)

                def groups(body, n):
                    for k in range(n):
                        for lane in range(2):
                            load_raw(lane, (U, V)[lane], l, body * 2 + (k + 1), body * 2 + (l * GROUPS + k + 1))

                with sp.Fori(AHEAD // 2, BODIES - 2) as body:
                    groups(body, 2)
                    next_g(body)
                groups(BODIES - 2, 2)
                groups(BODIES - 1, 1)
                sp.wait_ge(mm_done, EXPERT_END[l] - KD)
                sp.dma_start(X[:, :, :].rearrange("p k t -> p (k t)"), x_dram).then_inc(x_back, 16)
            for k in range(KD):
                sp.wait_ge(y_ready, k + 1)
                sp.dma_start(out_y[:, k, :], H[:, k, :]).then_inc(y_out, 16)
            sp.wait_ge(y_out, 16 * KD)
            sp.wait_ge(state_out, 16 * 6)

        @block.tensor
        def _(pe):
            w, slot, wts, sub, lanes = Walk(), Count(), Count(2), Count(), (Count(), Count())
            last = [None] * PAIRS

            def begin(reader):
                pair = w.use.n % PAIRS
                if last[pair] is not None:
                    who, value = last[pair]
                    pe.wait_ge(act_read if who == "act" else dve_read, value)
                u = w.take(reader)
                last[pair] = (reader, (w.act if reader == "act" else w.dve).at())
                return u

            def drained():
                for who, count in ((act_read, w.act), (dve_read, w.dve)):
                    if count.n:
                        pe.wait_ge(who, count.at())

            def from_turn_before(reader):
                count = w.act if reader == "act" else w.dve
                for i in range(PAIRS):
                    last[(w.use.n + i) % PAIRS] = (reader, count.at(i - PAIRS + 1))

            def slot_ready():
                pe.wait_ge(slot_in[slot.n % RING], slot.over(RING) * 16 + 16)
                slot.n += 1
                return ring[:, (slot.n - 1) % RING, :]

            def project(slots, src, readers, ready):
                for s in range(slots):
                    wt = slot_ready()
                    for m in range(4):
                        u = begin(readers[4 * s + m])
                        for k in range(KD):
                            if s == 0 and m == 0:
                                ready(k)
                            for a, b, _ in SEG:
                                mm = pe.matmul(ps(u)[:, a:b], wt[:, k * 512 + m * P:k * 512 + (m + 1) * P], src[:, k, a:b],
                                               start=(k == 0), stop=(k == KD - 1))
                        mm.then_inc(mm_done, 1)

            def column_sums(src, chunks, semaphore, value, gap=0):
                u = begin("dve")
                for k in range(chunks):
                    pe.wait_ge(semaphore, value + k)
                    for a, b, s in SEG:
                        mm = pe.matmul(ps(u)[:, a:b], ones[:, :], src[:, k, a + s * gap:b + s * gap],
                                       start=(k == 0), stop=(k == chunks - 1))
                mm.then_inc(mm_done, 1)

            def ada_slots():
                copied = {}
                for which, s in ORDER:
                    if which == 1:
                        wt = slot_ready()
                        u = begin("act")
                        copied[s] = w.act.at()
                        for k in range(KD):
                            mm = pe.matmul(PS[0:2, u % PAIRS, 0:512], cact[:, k, :], wt[:, k * 512:(k + 1) * 512],
                                           start=(k == 0), stop=(k == KD - 1))
                    else:
                        u = begin("act")
                        pe.wait_ge(act_read, copied[s])
                        for m in range(4):
                            mm = pe.matmul(ps(u)[:, 2 * m:2 * m + 2], mod_rows[:, s % 2, m * P:(m + 1) * P], ident[0:2, 0:2],
                                           start=True, stop=True)
                    mm.then_inc(mm_done, 1)

            def ada(turns):
                drained()
                with loop(pe, turns, *w.steps(act=8), (slot, 4)):
                    from_turn_before("act")
                    ada_slots()
                from_turn_before("act")

            def u_group(lane):
                pe.wait_ge(split[lane], lanes[lane].at(1))
                for j in range(4):
                    u = begin("act")
                    for k in range(KD):
                        for n, (pu, ph) in enumerate(PASSES):
                            for half in range(2):
                                mm = pe.matmul(ps_halves(u)[:, half, :], parts[lane][:, pu, k * 512 + j * P:k * 512 + (j + 1) * P],
                                               H16[:, ph, k, half * HALF:(half + 1) * HALF],
                                               start=(k == n == 0), stop=(k == KD - 1 and n == 2))
                    mm.then_inc(mm_done, 1)
                lanes[lane].n += 1

            def v_group(lane, grp):
                pe.wait_ge(split[lane], lanes[lane].at(1))
                for c in range(KD):
                    u = begin("dve")
                    for j in range(4):
                        if c == 0:
                            pe.wait_ge(w_ready, wts.at(j + 1))
                        for n, (pv, pw) in enumerate(PASSES):
                            for half in range(2):
                                mm = pe.matmul(ps_halves(u)[:, half, :], parts[lane][:, pv, j * D + c * P:j * D + (c + 1) * P],
                                               WT[:, grp, pw, j, half * HALF:(half + 1) * HALF],
                                               start=(j == n == 0), stop=(j == 3 and n == 2))
                    mm.then_inc(mm_done, 1)
                wts.n += 4
                lanes[lane].n += 1

            pe.wait_ge(consts_made, CONSTS)
            pe.wait_ge(cact_ready, 1)
            for l in range(LAYERS):
                if l == 0:
                    ada_slots()
                    ada(ADA_SLOTS // 4 - 1)
                column_sums(H, KD, sq_ready, NORM[2 * l] + 1)
                project(IN_SLOTS[l], H, ["act"] * 12 if l == 0 else ["act"] * 16 + ["dve"] * 8,
                        lambda k: pe.wait_ge(h_ready, 2 * KD * l + k + 1))
                if l == 0:
                    pe.wait_ge(pool_in, 16)
                    for g in range(KA):
                        pe.wait_ge(pooled, g + 1)
                        u = begin("act")
                        for a, b, _ in SEG:
                            mm = pe.matmul(ps(u)[:, a:b], wpool[:, g, :], PL[:, g, a:b], start=True, stop=True)
                        mm.then_inc(mm_done, 1)
                    branch = w.act.at()
                    ada(ADA_SLOTS // 4)
                    column_sums(CONV, KA, conv_ready, 1, EA_PAD)
                    column_sums(SQ, KA, sq_ready, KD + 1)
                    project(OUT_SLOTS, Z, ["dve"] * 8,
                            lambda k: pe.wait_ge(z_ready, k + 1) if k < KA else pe.wait_ge(act_read, branch))
                else:
                    project(OUT_SLOTS, Z, ["dve"] * 8, lambda k: pe.wait_ge(z_ready, KA + k + 1))
                column_sums(H, KD, sq_ready, NORM[2 * l + 1] + 1)
                project(Q_SLOTS, H, ["act"] * NQ, lambda k: pe.wait_ge(h_ready, 2 * KD * l + KD + k + 1))

                pe.wait_ge(keys_in, 16 * (l + 1))
                pe.wait_ge(act_read, w.act.at())
                for t in range(5):
                    n = P if t < 4 else NS_
                    for j in range(2):
                        u = begin("dve")
                        for q in range(8):
                            mm = pe.matmul(PS[0:n, u % PAIRS, q * P:(q + 1) * P], QT[:, 8 * j + q, t * P:t * P + n],
                                           keyT[:, 8 * j + q, :], start=True, stop=True)
                        mm.then_inc(mm_done, 1)
                    pe.wait_ge(h_split, KD * (l + 1))
                    for lane in range(2):
                        u_group(lane)
                    pe.wait_ge(keys_found, l * 5 + t + 1)
                    u = begin("act")
                    for j in range(2):
                        mm = pe.transpose(ps(u)[:, j * P:(j + 1) * P], KEYS[:, j, :], ident[:, :])
                    mm.then_inc(mm_done, 1)
                    pe.wait_ge(gates_ready, l * 5 + t + 1)
                    u = begin("act")
                    pe.transpose(ps(u, P), GG.rearrange("p h k -> p (h k)"), ident[:, :]).then_inc(mm_done, 1)
                    drained()
                    with loop(pe, 4 if t < 4 else 1, *w.steps(act=4), (sub, 4)):
                        from_turn_before("act")
                        for s in range(4):
                            u = begin("act")
                            pe.wait_ge(o1_ready, sub.at(s + 1))
                            pe.wait_ge(weighted, sub.at(s + 1))
                            for i in range(SUB):
                                mm = pe.matmul(ps(u, 1024)[:, i * P:(i + 1) * P], O2[:, s % 2, i, :], O1[:, s % 2, i, :],
                                               start=True, stop=True)
                            mm.then_inc(mm_done, 1)
                        sub.n += 4
                    from_turn_before("act")

                drained()
                with loop(pe, AHEAD // 2, *w.steps(dve=16), (lanes[0], 1), (lanes[1], 1), (wts, 8)):
                    from_turn_before("dve")
                    for grp in range(2):
                        v_group(grp, grp)
                drained()
                with loop(pe, BODIES - AHEAD // 2, *w.steps(act=8, dve=16), (lanes[0], 2), (lanes[1], 2), (wts, 8)):
                    from_turn_before("dve")
                    for grp in range(2):
                        u_group(0)
                        v_group(1, grp)
                from_turn_before("dve")
            column_sums(H, KD, sq_ready, NORM[4] + 1)

        @block.scalar
        def _(act):
            w, body, wts, lanes = Walk(), Count(1), Count(2), (Count(), Count())

            def next_use():
                act.wait_ge(mm_done, w.use.at(1))
                return w.take("act")

            def squares(src, dst, chunks, semaphore, value):
                for k in range(chunks):
                    act.wait_ge(semaphore, value + k)
                    act.activation(dst[:, k, :], src[:, k, :], ACT.Square).then_inc(sq_ready, 1)

            def root():
                w.take("dve")
                act.wait_ge(dve_read, w.dve.at())
                act.activation(stat[:, 1, :], stat[:, 0, :], ACT.Sqrt).then_inc(std_ready, 1)

            def modulate(l, which):
                sh = mod_at["sh1" if which == 0 else "sh2"] * KD
                for k in range(KD):
                    act.wait_ge(xn_ready, NORM[2 * l + which] + k + 1)
                    for a, b, s in SEG:
                        ins = act.activation(H[:, k, a:b], H[:, k, a:b], ACT.Identity,
                                             scale=scale[:, l, which, k, s:s + 1], bias=mod[:, l, sh + k, s:s + 1])
                    ins.then_inc(h_ready, 1)

            def store_state(dst, src):
                act.dma_start(dst, src).then_inc(state_out, 16)

            act.dma_start(EA[:, :, EA_PAD + NP_:2 * EA_PAD + NP_], state_a).then_inc(state_in, 16)
            act.dma_start(EB[:, :, EB_PAD + NP_:2 * EB_PAD + NP_], state_b).then_inc(state_in, 16)
            act.dma_start(wpool[:, :, :], w_pool).then_inc(pool_in, 16)
            act.wait_ge(vec_in, 16)
            act.activation(cact[:, :, :].rearrange("p k s -> p (k s)"), vecs("c"), ACT.Sigmoid).then_inc(c_sigmoid, 1)

            def ada(l):
                with loop(act, ADA_SLOTS // 4, *w.steps(act=8)) as turn:
                    for which, s in ORDER:
                        u = next_use()
                        if which == 1:
                            act.copy(mod_rows[:, s % 2, :], PS[0:2, u % PAIRS, 0:512]).then_inc(act_read, 1)
                        else:
                            act.copy(mod[:, l, bass.ds(turn * 16 + 4 * s, 4), :],
                                     ps(u, 8).rearrange("p (m s) -> p m s", s=2)).then_inc(act_read, 1)

            for l in range(LAYERS):
                if l == 0:
                    act.wait_ge(x_in, 16)
                    for k in range(KD):
                        act.activation(H[:, k, :], X[:, k, :], ACT.Square).then_inc(sq_ready, 1)
                    ada(0)
                else:
                    squares(X, H, KD, x_ready, 1)
                root()
                act.wait_ge(mod_ready, l + 1)
                modulate(l, 0)
                if l == 0:
                    act.wait_ge(consts_made, CONSTS)
                    for c in range(KA):
                        u = next_use()
                        for a, b, s in SEG:
                            ins = act.copy(EA[:, c, a + EA_PAD * (1 + s):b + EA_PAD * (1 + s)], ps(u)[:, a:b])
                        ins.then_inc(act_read, 1)
                    for c in range(KA):
                        u = next_use()
                        if c >= 2:
                            act.wait_ge(glu_ready, c - 1)
                        act.activation(SG[:, c % 2, :], ps(u), ACT.Sigmoid).then_inc(act_read, 1)
                    for c in range(KA):
                        u = next_use()
                        for a, b, s in SEG:
                            ins = act.copy(EB[:, c, a + EB_PAD * (1 + s):b + EB_PAD * (1 + s)], ps(u)[:, a:b])
                        ins.then_inc(act_read, 1)
                    act.wait_ge(glu_ready, KA)
                    store_state(out_ap, EA[:, :, NP_:NP_ + EA_PAD])
                    store_state(out_as, EA[:, :, EA_W - EA_PAD:EA_W])
                    act.wait_ge(act_read, w.act.at())
                    store_state(out_bp, EB[:, :, NP_:NP_ + EB_PAD])
                    store_state(out_bs, EB[:, :, EB_W - EB_PAD:EB_W])
                    for g in range(KA):
                        u = next_use()
                        act.activation(Z[:, KA + g, :], ps(u), ACT.Identity,
                                       scale=vecs("pool_scale")[:, g:g + 1]).then_inc(act_read, 1)
                    ada(1)
                    w.take("dve")
                    squares(YC, SQ, KA, centered, 1)
                    root()
                    for k in range(KA):
                        act.wait_ge(xn_ready, KD + k + 1)
                        act.activation(SQ[:, k, :], YC[:, k, :], ACT.Sigmoid, scale=vecs("ln_a_g")[:, k:k + 1],
                                       bias=vecs("ln_a_b")[:, k:k + 1]).then_inc(ln_sig, 1)
                else:
                    act.wait_ge(x_ready, KD)
                    act.wait_ge(pads_made, 1)
                    act.wait_ge(c_in, 16)
                    for c in range(2 * KD):
                        u = next_use()
                        if c < KD:
                            act.copy(BG[:, c, :], ps(u)).then_inc(act_read, 1)
                        else:
                            for a, b, s in SEG:
                                ins = act.copy(EC[:, c - KD, a + EC_PAD * (1 + s):b + EC_PAD * (1 + s)], ps(u)[:, a:b])
                            ins.then_inc(act_read, 1)
                    w.take("dve", KD)
                    act.wait_ge(dve_read, w.dve.at())
                    store_state(out_cp, EC[:, :, NP_:NP_ + EC_PAD])
                    store_state(out_cs, EC[:, :, EC_W - EC_PAD:EC_W])
                w.take("dve", KD)
                squares(X, H, KD, dve_read, w.dve.at(1 - KD))
                root()
                modulate(l, 1)
                act.wait_ge(x_stored, 16 * (l + 1))
                for k in range(KD):
                    act.wait_ge(h_ready, 2 * KD * l + KD + k + 1)
                    act.copy(H16[:, 0, k, :], H[:, k, :]).then_inc(h_high, 1)
                act.wait_ge(state_out, (64, 96)[l])
                for c in range(NQ):
                    u = next_use()
                    act.copy(QT[:, c, :], ps(u)).then_inc(act_read, 1)

                def high(lane, scale):
                    lanes[lane].n += 1
                    act.wait_ge(raw_in[lane], lanes[lane].at() * 16)
                    act.wait_ge(mm_done, w.use.at())
                    act.activation(parts[lane][:, 0, :], raw[lane], ACT.Copy, scale=scale).then_inc(high_made[lane], 1)

                def gelu(dst):
                    u = next_use()
                    act.activation(dst.rearrange("p (b c) -> p b c", b=2), ps_halves(u), ACT.Gelu_apprx_tanh,
                                   scale=1.0 / U_SCALE).then_inc(act_read, 1)

                def tile_and_steps(t, steps, last_tile=False):
                    w.take("dve", 2)
                    act.wait_ge(act_stored[0], t * 16 + 16)
                    for j in range(4):
                        gelu(ahead[:, 0, j, :])
                    if not last_tile:
                        high(0, U_SCALE)
                    act.wait_ge(act_stored[1], t * 16 + 16)
                    for j in range(4):
                        if j == 2:
                            act.wait_ge(shifted, t + 1)
                            act.activation(GG, GG, ACT.Exp).then_inc(exped, 1)
                        gelu(ahead[:, 1, j, :])
                    u = next_use()
                    act.copy(IT.rearrange("p j t -> p (j t)"), ps(u, 2 * P)).then_inc(act_read, 1)
                    u = next_use()
                    act.copy(GT, ps(u, P)).then_inc(act_read, 1)
                    if not last_tile:
                        high(1, U_SCALE)
                    with loop(act, steps, *w.steps(act=4), (body, 1)):
                        for s in range(4):
                            if s % 2 == 0:
                                act.wait_ge(g_written[s // 2], body.at() * 16)
                            u = next_use()
                            dst = stage[:, s // 2, :, SUB * (s % 2):SUB * (s % 2) + SUB, :]
                            act.copy(dst, ps(u, 1024).rearrange("p (t g e) -> p g t e", t=SUB, e=8)).then_inc(act_read, 1)
                        body.n += 1

                for lane in range(2):
                    high(lane, U_SCALE)
                with loop(act, TILES - 1, (w.use, 28), (w.act, 26), (w.dve, 2), (body, 4),
                          (lanes[0], 1), (lanes[1], 1)) as turn:
                    tile_and_steps(turn + TILES * l, 4)
                tile_and_steps(TILES * l + TILES - 1, 1, True)

                high(0, 1.0)
                with loop(act, AHEAD // 2 - 1, *w.steps(dve=16), (lanes[0], 1), (lanes[1], 1)):
                    for lane in (1, 0):
                        high(lane, 1.0)
                        w.take("dve", KD)
                high(1, 1.0)
                w.take("dve", KD)
                high(0, U_SCALE)
                w.take("dve", KD)
                wts.n += 4 * AHEAD

                def expert_body(groups_ahead):
                    for grp in range(2):
                        high(1, 1.0)
                        for j in range(4):
                            act.wait_ge(w_ready, wts.at(j - 1))
                            gelu(AG[:, j % 2, :])
                        wts.n += 4
                        if grp < groups_ahead:
                            high(0, U_SCALE)
                        w.take("dve", KD)

                with loop(act, BODIES - AHEAD // 2 - 1, *w.steps(act=8, dve=16), (wts, 8), (lanes[0], 2), (lanes[1], 2)):
                    expert_body(2)
                expert_body(1)
            act.wait_ge(x_back, 16 * LAYERS)
            squares(X, H, KD, x_ready, KD + 1)
            root()

        @block.gpsimd
        def _(pool):
            w, sub = Walk(), Count()
            steps = 0

            def link(ins):
                nonlocal steps
                steps += 1
                ins.then_inc(pool_step, 1)
                pool.wait_ge(pool_step, steps)

            pool.memset(ones[:, :], 1.0).then_inc(consts_made, 1)
            link(pool.memset(ident[:, :], 0.0))
            pool.affine_select(out=ident[:, :], in_=ident[:, :], compare_op=ALU.not_equal, fill=1.0, base=0,
                               pattern=[[-1, P]], channel_multiplier=1).then_inc(consts_made, 1)
            pool.iota(iota[:, :], [[1, P]], base=0, channel_multiplier=0,
                      allow_small_or_imprecise_dtypes=True).then_inc(consts_made, 1)
            for i in range(PB + 1):
                ins = pool.memset(inv_count[:, i:i + 1], 1.0 / (i + 1))
            link(ins)
            pool.memset(EA[:, :, 0:EA_PAD], 0.0).then_inc(consts_made, 1)
            pool.memset(EB[:, :, 0:EB_PAD], 0.0).then_inc(consts_made, 1)
            for l in range(LAYERS):
                if l == 0:
                    w.take("act", 2 * ADA_SLOTS)
                w.take("dve")
                if l == 0:
                    pool.wait_ge(state_in, 32)
                    pool.wait_ge(consts_made, CONSTS)
                    w.take("act", 2 * KA)
                    for g, wnd in enumerate(WINDOWS):
                        w.take("act")
                        pool.wait_ge(act_read, w.act.at())
                        src, have = EB[:, g, :], 1
                        for i in range(g + 1):
                            dst = PT[:, i % 2, :]
                            link(pool.tensor_tensor(dst[:, 2 * have - 1:EB_W], src[:, 2 * have - 1:EB_W],
                                                    src[:, have - 1:EB_W - have], ALU.add))
                            src, have = dst, 2 * have
                        for a, b, s in SEG:
                            o = EB_PAD * (1 + s)
                            link(pool.tensor_scalar(PL[:, g, a:b], src[:, a + o:b + o], 1.0 / wnd, None, ALU.mult))
                        link(pool.tensor_tensor(PL[:, g, 0:wnd], src[:, EB_PAD:EB_PAD + wnd], inv_count[:, 0:wnd], ALU.mult))
                        for a, b, s in SEG:
                            o = EB_PAD * (1 + s)
                            ins = pool.tensor_tensor(PL[:, g, a:b], PL[:, g, a:b], EB[:, g, a + o:b + o], ALU.subtract)
                        ins.then_inc(pooled, 1)
                    w.take("act", KA + 2 * ADA_SLOTS)
                    w.take("dve", 2)
                else:
                    pool.wait_ge(x_ready, KD)
                    pool.memset(EC[:, :, 0:EC_PAD], 0.0).then_inc(pads_made, 1)
                    pool.dma_start(EC[:, :, EC_PAD + NP_:2 * EC_PAD + NP_], state_c).then_inc(c_in, 16)
                    w.take("act", 2 * KD)
                    w.take("dve", KD)
                w.take("dve", KD + 1)
                w.take("act", NQ)

                def tile_and_steps(steps):
                    w.take("dve", 2)
                    w.take("act", 10)
                    transposed = w.act.at()
                    with loop(pool, steps, *w.steps(act=4), (sub, 4)) as turn:
                        pool.wait_ge(act_read, transposed)
                        for s in range(4):
                            tok = bass.ds(turn * STEP + SUB * s, SUB)
                            pool.wait_ge(o2_ready, sub.at(s + 1))
                            pool.tensor_tensor(O2[:, s % 2, :, :], O2[:, s % 2, :, :],
                                               GT[:, tok].unsqueeze(2).to_broadcast([P, SUB, P]), ALU.mult).then_inc(weighted, 1)
                        w.take("act", 4)
                        sub.n += 4

                with loop(pool, 4, (w.use, 28), (w.act, 26), (w.dve, 2), (sub, 16)):
                    tile_and_steps(4)
                tile_and_steps(1)
                for s in range(2):
                    pool.wait_ge(g_written[s], 16 * ((l + 1) * STEPS + 1))
                pool.memset(ACCF[:, :], 0.0).then_inc(acc_zero, 1)
                w.take("act", 4 * (GROUPS - AHEAD))
                w.take("dve", 8 * GROUPS)

        @block.vector
        def _(dve):
            w, step, sub, lanes, wf = Walk(), Count(), Count(), (Count(), Count()), Count()
            carried = [0]

            def next_use():
                dve.wait_ge(mm_done, w.use.at(1))
                return w.take("dve")

            def link(ins):
                ins.then_inc(dve_step, 1)
                step.n += 1
                settle(dve_step, step.at())

            def settle(semaphore, value):
                dve.wait_ge(semaphore, value)
                if not isinstance(value, int):
                    carried[0] += 1
                    dve.memset(carrier[:, carried[0] % 3:carried[0] % 3 + 1], 0.0)

            def inverse_root(n, width):
                u = next_use()
                dve.tensor_scalar(stat[:, 0, :], ps(u), 1.0 / width, EPS, ALU.mult, ALU.add).then_inc(dve_read, 1)
                dve.wait_ge(std_ready, n)
                link(dve.reciprocal(stat[:, 2, :], stat[:, 1, :]))
                link(dve.tensor_tensor(stat[:, 1, :], stat[:, 0, :], stat[:, 2, :], ALU.mult))
                link(dve.tensor_tensor(stat[:, 1, :], stat[:, 1, :], stat[:, 2, :], ALU.mult))
                link(dve.tensor_scalar(stat[:, 1, :], stat[:, 1, :], -0.5, 1.5, ALU.mult, ALU.add))
                link(dve.tensor_tensor(stat[:, 2, :], stat[:, 1, :], stat[:, 2, :], ALU.mult))

            def norm_x(n):
                inverse_root(n, D)
                for k in range(KD):
                    dve.tensor_tensor(H[:, k, :], X[:, k, :], stat[:, 2, :], ALU.mult).then_inc(xn_ready, 1)

            def residual(l, gate, experts):
                for k in range(KD):
                    u = None if experts else next_use()
                    for a, b, s in SEG:
                        y = ACC[:, k, a:b] if experts else ps(u)[:, a:b]
                        ins = dve.scalar_tensor_tensor(out=X[:, k, a:b], in0=y, scalar=mod[:, l, mod_at[gate] * KD + k, s:s + 1],
                                                       in1=X[:, k, a:b], op0=ALU.mult, op1=ALU.add)
                    ins.then_inc(x_ready if experts else dve_read, 1)
                dve.wait_ge(x_ready if experts else dve_read, KD * (l + 1) if experts else w.dve.at())

            for i in range(2):
                dve.memset(carrier[:, i:i + 1], 0.0).then_inc(w_ready, 1)
            dve.wait_ge(vec_in, 16)
            dve.wait_ge(c_sigmoid, 1)
            flat = cact[:, :, :].rearrange("p k s -> p (k s)")
            dve.tensor_tensor(flat, flat, vecs("c"), ALU.mult).then_inc(cact_ready, 1)
            dve.wait_ge(consts_made, CONSTS)
            dve.wait_ge(x_in, 16)
            for l in range(LAYERS):
                if l == 0:
                    w.take("act", 2 * ADA_SLOTS)
                    ada_done = w.act.at()
                dve.wait_ge(act_read, ada_done)
                bias = vecs("b_ada")[:, l * 6 * KD:(l + 1) * 6 * KD]
                link(dve.tensor_tensor(mod[:, l, :, :], mod[:, l, :, :], bias.unsqueeze(2).to_broadcast([P, 6 * KD, 2]), ALU.add))
                for which, (sc, g) in enumerate((("sc1", "norm_mix_g"), ("sc2", "norm_ffn_g"))):
                    at = mod_at[sc] * KD
                    gv = vecs(g)[:, l * KD:(l + 1) * KD].unsqueeze(2).to_broadcast([P, KD, 2])
                    link(dve.tensor_scalar(scale[:, l, which, :, :], mod[:, l, at:at + KD, :], 1.0, None, ALU.add))
                    ins = dve.tensor_tensor(scale[:, l, which, :, :], scale[:, l, which, :, :], gv, ALU.mult)
                at = mod_at["g2"] * KD
                link(ins)
                dve.tensor_scalar(mod[:, l, at:at + KD, :], mod[:, l, at:at + KD, :], 1.0 / W_SCALE, None,
                                  ALU.mult).then_inc(mod_ready, 1)
                norm_x((1, 4)[l])
                if l == 0:
                    dve.wait_ge(state_in, 32)
                    w.take("act", KA)
                    for c in range(KA):
                        w.take("act")
                        dve.wait_ge(act_read, w.act.at())
                        for a, b, s in SEG:
                            o = EA_PAD * (1 + s)
                            ins = dve.tensor_tensor(EA[:, c, a + o:b + o], EA[:, c, a + o:b + o], SG[:, c % 2, a:b], ALU.mult)
                        ins.then_inc(glu_ready, 1)
                    w.take("act", 2 * KA + 2 * ADA_SLOTS)
                    ada_done = w.act.at()
                    dve.wait_ge(glu_ready, KA)
                    wide = T + EA_PAD
                    for i in range(WA):
                        for c in range(KA):
                            tap = vecs("dw_a")[:, c * WA + i:c * WA + i + 1]
                            if i == 0:
                                ins = dve.tensor_scalar(CONV[:, c, :], EA[:, c, 0:wide], tap, vecs("db_a")[:, c:c + 1],
                                                        ALU.mult, ALU.add)
                            else:
                                dve.wait_ge(dve_step, step.n - (KA - 1 if i < WA - 1 else KA - 1 - c))
                                ins = dve.scalar_tensor_tensor(out=CONV[:, c, :], in0=EA[:, c, i:i + wide], scalar=tap,
                                                               in1=CONV[:, c, :], op0=ALU.mult, op1=ALU.add)
                            if i < WA - 1:
                                ins.then_inc(dve_step, 1)
                                step.n += 1
                            else:
                                ins.then_inc(conv_ready, 1)
                    dve.wait_ge(conv_ready, KA)
                    u = next_use()
                    for k in range(KA):
                        for a, b, s in SEG:
                            ins = dve.scalar_tensor_tensor(out=YC[:, k, a:b], in0=ps(u)[:, a:b], scalar=-1.0 / DA,
                                                           in1=CONV[:, k, a + s * EA_PAD:b + s * EA_PAD],
                                                           op0=ALU.mult, op1=ALU.add)
                        ins.then_inc(centered, 1)
                    dve.wait_ge(centered, KA)
                    dve.tensor_copy(carrier[:, 3:4], ps(u, 1)).then_inc(dve_read, 1)
                    inverse_root(2, DA)
                    for k in range(KA):
                        dve.tensor_tensor(YC[:, k, :], YC[:, k, :], stat[:, 2, :], ALU.mult).then_inc(xn_ready, 1)
                    for k in range(KA):
                        dve.wait_ge(ln_sig, k + 1)
                        link(dve.tensor_scalar(YC[:, k, :], YC[:, k, :], vecs("ln_a_g")[:, k:k + 1],
                                               vecs("ln_a_b")[:, k:k + 1], ALU.mult, ALU.add))
                        dve.tensor_tensor(Z[:, k, :], YC[:, k, :], SQ[:, k, :], ALU.mult).then_inc(z_ready, 1)
                else:
                    w.take("act", KD)
                    wide = T + EC_PAD
                    first = w.act.n
                    w.take("act", KD)
                    for c in range(KD):
                        dve.wait_ge(act_read, first + c + 1)
                        u = next_use()
                        for a, b, s in SEG:
                            o = EC_PAD * (1 + s)
                            ins = dve.tensor_tensor(EC[:, c, a + o:b + o], ps(u)[:, a:b], EC[:, c, a + o:b + o], ALU.mult)
                        ins.then_inc(dve_read, 1)
                        dve.wait_ge(dve_read, w.dve.at())
                        dve.wait_ge(pads_made, 1)
                        dve.wait_ge(c_in, 16)
                        for i in range(WC):
                            tap = vecs("dw_c")[:, c * WC + i:c * WC + i + 1]
                            if i == 0:
                                link(dve.tensor_scalar(YO[:, c, 0:wide], EC[:, c, 0:wide], tap, None, ALU.mult))
                            else:
                                link(dve.scalar_tensor_tensor(out=YO[:, c, 0:wide], in0=EC[:, c, i:i + wide], scalar=tap,
                                                              in1=YO[:, c, 0:wide], op0=ALU.mult, op1=ALU.add))
                        for a, b, s in SEG:
                            o = EC_PAD * s
                            ins = dve.tensor_tensor(Z[:, c, a:b], YO[:, c, a + o:b + o], BG[:, c, a:b], ALU.mult)
                        ins.then_inc(z_ready, 1)
                residual(l, "g1", False)
                norm_x((3, 5)[l])
                w.take("act", NQ)

                for k in range(KD):
                    dve.wait_ge(h_high, l * KD + k + 1)
                    dve.tensor_tensor(H16[:, 1, k, :], H[:, k, :], H16[:, 0, k, :], ALU.subtract).then_inc(h_split, 1)

                def low(lane, scale):
                    lanes[lane].n += 1
                    dve.wait_ge(high_made[lane], lanes[lane].at())
                    dve.scalar_tensor_tensor(out=parts[lane][:, 1, :], in0=raw[lane], scalar=scale, in1=parts[lane][:, 0, :],
                                             op0=ALU.mult, op1=ALU.subtract).then_inc(split[lane], 1)

                def tile_and_steps(t, steps, last_tile=False):
                    low(1, U_SCALE)
                    uu = [next_use(), next_use()]
                    settle(mm_done, w.use.at())

                    def score(q):
                        return PS[:, uu[q // 8] % PAIRS, (q % 8) * P:(q % 8 + 1) * P]

                    def best(q, lo):
                        return V16[:, q // 2, q % 2, lo:lo + 8]

                    for q in range(NQ):
                        ins = dve.max(best(q, 0), score(q))
                    link(ins)
                    for q in range(NQ):
                        dve.max_index(I16[:, q // 2, q % 2, 0:8], best(q, 0), score(q))
                        ins = dve.match_replace(ZT[:, q, :], best(q, 0), score(q), NEG)
                        if q % 8 == 7:
                            ins.then_inc(dve_read, 1)
                    settle(dve_read, w.dve.at())
                    for q in range(NQ):
                        ins = dve.max(best(q, 8), ZT[:, q, :])
                    link(ins)
                    for q in range(NQ):
                        ins = dve.max_index(I16[:, q // 2, q % 2, 8:16], best(q, 8), ZT[:, q, :])
                    link(ins)
                    shape = [P, HEADS, TOPK, TOPK]
                    link(dve.tensor_tensor(CAND.rearrange("p h (a b) -> p h a b", a=TOPK),
                                           V16[:, :, 0, :].unsqueeze(3).to_broadcast(shape),
                                           V16[:, :, 1, :].unsqueeze(2).to_broadcast(shape), ALU.add))
                    for h in range(HEADS):
                        ins = dve.max(C8[:, h, 0:8], CAND[:, h, :])
                    link(ins)
                    for h in range(HEADS):
                        dve.max_index(P8[:, h, 0:8], C8[:, h, 0:8], CAND[:, h, :])
                        ins = dve.match_replace(ZAP[:, h, :], C8[:, h, 0:8], CAND[:, h, :], NEG)
                    link(ins)
                    for h in range(HEADS):
                        ins = dve.max(C8[:, h, 8:16], ZAP[:, h, :])
                    link(ins)
                    dve.tensor_tensor(GG, C8, C8[:, :, 0:1].to_broadcast([P, HEADS, TOPK]), ALU.subtract).then_inc(shifted, 1)
                    if not last_tile:
                        low(0, U_SCALE)
                    for h in range(HEADS):
                        ins = dve.max_index(P8[:, h, 8:16], C8[:, h, 8:16], ZAP[:, h, :])
                    link(ins)
                    flat = P8.rearrange("p h k -> p (h k)")
                    dve.tensor_scalar(PLACE[:, 0, :], flat, 4, None, ALU.logical_shift_right)
                    link(dve.tensor_scalar(PLACE[:, 1, :], flat, TOPK - 1, None, ALU.bitwise_and))
                    dve.tensor_copy(IF, I16)
                    link(dve.tensor_copy(PLF, PLACE))
                    for j in range(2):
                        link(dve.tensor_tensor(PICK, PLF[:, j, :].unsqueeze(2).to_broadcast([P, P, TOPK]),
                                               iota[:, 0:TOPK].unsqueeze(1).to_broadcast([P, P, TOPK]), ALU.is_equal))
                        pick = PICK.rearrange("p (h r) a -> p h r a", h=HEADS)
                        link(dve.tensor_tensor(pick, pick, IF[:, :, j, :].unsqueeze(2).to_broadcast(shape), ALU.mult))
                        ins = dve.tensor_reduce(KEYS[:, j, :], PICK, AX.X, ALU.add)
                        if j == 0:
                            link(ins)
                    ins.then_inc(keys_found, 1)
                    dve.wait_ge(exped, t + 1)
                    link(dve.tensor_reduce(ZS, GG, AX.X, ALU.add))
                    link(dve.reciprocal(RZ, ZS))
                    dve.tensor_tensor(GG, GG, RZ.unsqueeze(2).to_broadcast([P, HEADS, TOPK]), ALU.mult).then_inc(gates_ready, 1)
                    w.take("act", 10)
                    transposed = w.act.at()
                    with loop(dve, steps, *w.steps(act=4), (sub, 4)) as turn:
                        dve.wait_ge(act_read, transposed)
                        for s in range(4):
                            tok = bass.ds(turn * STEP + SUB * s, SUB)
                            dve.wait_ge(mm_done, w.use.at(s - 1))
                            for rows, key, ready in ((O2, 1, o2_ready), (O1, 0, o1_ready)):
                                dve.tensor_tensor(rows[:, s % 2, :, :], iota[:, :].unsqueeze(1).to_broadcast([P, SUB, P]),
                                                  IT[:, key, tok].unsqueeze(2).to_broadcast([P, SUB, P]),
                                                  ALU.is_equal).then_inc(ready, 1)
                        w.take("act", 4)
                        sub.n += 4

                low(0, U_SCALE)
                with loop(dve, TILES - 1, (w.use, 28), (w.act, 26), (w.dve, 2), (sub, 16), (step, TILE_LINKS),
                          (lanes[0], 1), (lanes[1], 1)) as turn:
                    tile_and_steps(turn + TILES * l, 4)
                tile_and_steps(TILES * l + TILES - 1, 1, True)

                def gates_of(body):
                    at = slice((body % 2) * T * 8, (body % 2 + 1) * T * 8) if isinstance(body, int) else \
                        bass.ds((body % 2) * (T * 8), T * 8)
                    return GB[:, at].rearrange("p (t e) -> p t e", e=8)

                def weigh(a, gate, grp, j):
                    wf.n += 1
                    dve.tensor_tensor(a, a, gate, ALU.mult).then_inc(wf_ready, 1)
                    dve.wait_ge(wf_ready, wf.at())
                    dve.tensor_scalar(WT[:, grp, 0, j, :], a, W_SCALE, None, ALU.mult).then_inc(w_high, 1)
                    dve.wait_ge(w_high, wf.at())
                    dve.scalar_tensor_tensor(out=WT[:, grp, 1, j, :], in0=a, scalar=W_SCALE, in1=WT[:, grp, 0, j, :],
                                             op0=ALU.mult, op1=ALU.subtract).then_inc(w_ready, 1)

                def add(c):
                    dve.wait_ge(dve_read, w.dve.at(1 - KD))
                    u = next_use()
                    acc = ACC[:, c, :].rearrange("p (b c) -> p b c", b=2)
                    dve.tensor_tensor(acc, ps_halves(u), acc, ALU.add).then_inc(dve_read, 1)

                def add_and_prepare(body, lane, scale, more=True):
                    done = w.use.at()
                    for c in range(KD):
                        add(c)
                        if c == 0:
                            low(lane, scale)
                        if more and c in (1, 3, 5, 6):
                            j = (1, 3, 5, 6).index(c)
                            if j == 0:
                                dve.wait_ge(act_in[lane], act_turn(body, lane))
                                dve.wait_ge(g_in, (body + (1 - lane)) * 16 + 16 * (l * BODIES + 1))
                                dve.wait_ge(mm_done, done)
                            weigh(AB[:, lane, j, :], gates_of(body + (1 - lane))[:, :, 4 * lane + j], lane, j)

                def act_turn(body, lane):
                    return (body + (2 - lane)) * 16 + 16 * l * (AHEAD // 2)

                low(0, 1.0)
                dve.wait_ge(acc_zero, l + 1)
                dve.wait_ge(act_in[0], 16 * (l * (AHEAD // 2) + 1))
                dve.wait_ge(g_in, 16 * (l * BODIES + 1))
                for j in range(4):
                    weigh(AB[:, 0, j, :], gates_of(0)[:, :, j], 0, j)
                with loop(dve, AHEAD // 2 - 1, *w.steps(dve=16), (wf, 8), (lanes[0], 1), (lanes[1], 1)) as turn:
                    add_and_prepare(turn, 1, 1.0)
                    add_and_prepare(turn, 0, 1.0)
                add_and_prepare(AHEAD // 2 - 1, 1, 1.0)
                add_and_prepare(AHEAD // 2 - 1, 0, U_SCALE, False)

                def expert_body(turn, groups_ahead):
                    dve.wait_ge(g_in, turn * 16 + 16 * (l * BODIES + 1))
                    g = gates_of(turn)
                    for grp in range(2):
                        low(1, 1.0)
                        dve.wait_ge(mm_done, w.use.at(-8))
                        for j in range(4):
                            w.take("act")
                            dve.wait_ge(act_read, w.act.at())
                            weigh(AG[:, j % 2, :], g[:, :, 4 * grp + j], grp, j)
                        if grp < groups_ahead:
                            low(0, U_SCALE)
                        for c in range(KD):
                            add(c)

                with loop(dve, BODIES - AHEAD // 2 - 1, *w.steps(act=8, dve=16), (wf, 8), (lanes[0], 2), (lanes[1], 2)) as turn:
                    expert_body(turn + AHEAD // 2, 2)
                expert_body(BODIES - 1, 1)
                dve.wait_ge(x_back, 16 * (l + 1))
                dve.wait_ge(dve_read, w.dve.at())
                residual(l, "g2", True)
            inverse_root(6, D)
            for k in range(KD):
                dve.scalar_tensor_tensor(out=H[:, k, :], in0=X[:, k, :], scalar=vecs("final_g")[:, k:k + 1],
                                         in1=stat[:, 2, :], op0=ALU.mult, op1=ALU.mult).then_inc(y_ready, 1)


def kernel(**inputs):
    import concourse.bacc as _bacc
    from concourse.bass_utils import run_bass_kernel_spmd as _run

    x = {k: np.asarray(v) for k, v in inputs.items()}

    def chunks(a):
        n, f = a.shape
        return np.ascontiguousarray(a.T.reshape(f // P, P, n).transpose(1, 0, 2))

    def slots(wt):
        k, m = wt.shape
        return wt.reshape(k // P, P, m // 512, 512).transpose(2, 1, 0, 3).reshape(m // 512, P, SLOT)

    def u_slots(u):
        return u.reshape(GROUPS, 512, KD, P).transpose(0, 3, 2, 1).reshape(GROUPS, P, SLOT)

    def v_slots(v):
        return v.reshape(GROUPS, 4, P, D).transpose(0, 2, 1, 3).reshape(GROUPS, P, SLOT)

    cols = {
        "norm_mix_g": x["norm_mix_g"].reshape(-1, P).T,
        "norm_ffn_g": x["norm_ffn_g"].reshape(-1, P).T,
        "b_ada": x["b_ada"].reshape(-1, P).T,
        "db_a": x["db_a"].reshape(-1, P).T,
        "ln_a_g": x["ln_a_g"].reshape(-1, P).T,
        "ln_a_b": x["ln_a_b"].reshape(-1, P).T,
        "pool_scale": x["pool_scale"].reshape(-1, P).T,
        "final_g": x["final_g"].reshape(-1, P).T,
        "dw_a": chunks(x["dw_a"][0]).reshape(P, -1),
        "dw_c": chunks(x["dw_c"][0]).reshape(P, -1),
        "c": chunks(np.concatenate([x["c_prompt"], x["c_sample"]])).reshape(P, -1),
    }
    front = [slots(w) for w in (x["w_ada"][0], x["w_in_even"][0], x["w_ada"][1], x["w_out_even"][0], x["peer_wq"][0],
                                x["w_in_odd"][0], x["w_out_odd"][0], x["peer_wq"][1])]
    keys = np.stack([x["peer_k1"], x["peer_k2"]], axis=2)
    arrays = {
        "xT": chunks(np.concatenate([x["x_prompt"][0], x["x_sample"][0]])),
        "vectors": np.concatenate([cols[name] for name, _ in VECTORS], axis=1),
        "state_a": chunks(x["state_conv_a"][0, 0]),
        "state_b": chunks(x["state_pool_b"][0, 0]),
        "state_c": chunks(x["state_conv_c"][0, 0]),
        "w_pool": x["w_pool"][0].transpose(1, 0, 2),
        "keys": keys.reshape(LAYERS, NQ, NKEYS, P).transpose(0, 3, 1, 2),
        "front_w": np.concatenate(front),
        "U": np.stack([u_slots(u) for u in x["peer_u"]]),
        "V": np.stack([v_slots(v) for v in x["peer_v"]]),
    }
    arrays = {k: np.ascontiguousarray(v) for k, v in arrays.items()}
    outs = {"y": (P, KD, T), "new_ap": (P, KA, EA_PAD), "new_as": (P, KA, EA_PAD), "new_bp": (P, KA, EB_PAD),
            "new_bs": (P, KA, EB_PAD), "new_cp": (P, KD, EC_PAD), "new_cs": (P, KD, EC_PAD)}
    nc = _bacc.Bacc("TRN2", target_bir_lowering=False, num_devices=1)
    args = [nc.dram_tensor(k, v.shape, F32, kind="ExternalInput").ap() for k, v in arrays.items()]
    args += [nc.dram_tensor(k, shape, F32, kind="ExternalOutput").ap() for k, shape in outs.items()]
    scratch = {"gates_dram": (P, BODIES, T, 8), "act_dram": (P, AHEAD, 4 * T), "x_dram": (P, KD * T)}
    args += [nc.dram_tensor(k, shape, F32, kind="Internal").ap() for k, shape in scratch.items()]
    build(nc, *args)
    r = _run(nc, [arrays], core_ids=[0]).results[0]

    def rows(a):
        a = np.asarray(a)
        return np.ascontiguousarray(a.transpose(2, 1, 0).reshape(a.shape[2], -1))

    y = rows(r["y"])
    new = [rows(r[k])[None, None] for k in ("new_ap", "new_bp", "new_cp", "new_as", "new_bs", "new_cs")]
    return (y[None, :NP_], y[None, NP_:], *new)
```

```python
from contextlib import ExitStack, contextmanager

import numpy as np

import concourse.bass as bass
from concourse import mybir

ALU = mybir.AluOpType
ACT = mybir.ActivationFunctionType
AX = mybir.AxisListType
F32 = mybir.dt.float32
F16 = mybir.dt.float16
U32 = mybir.dt.uint32

P = 128
D = 1024
KD = D // P
LAYERS = 2
NP_, NS_ = 512, 32
T = NP_ + NS_
HALF = T // 2
DA = 512
KA = DA // P
WA, WC = 31, 3
WINDOWS = (2, 4, 8, 16)
PB = max(WINDOWS) - 1
HEADS, NKEYS, TOPK = 8, 128, 16
NQ = 2 * HEADS
EPS = 1e-6
NEG = float(np.float32(-3.0e38))

SLOT = 4096
RING = 4
PAIRS = 4
U_SCALE, W_SCALE = 32.0, 16.0
GROUPS = NKEYS // 4
BODIES = GROUPS // 2
TILES = 5
AHEAD = 2 * (TILES + 1)
SUB = 8
STEP = 32
ADA_SLOTS, IN_SLOTS, OUT_SLOTS, Q_SLOTS = 12, (3, 6), 2, 4
BEFORE = ((3, 4), (3 + GROUPS + 5, 4 + GROUPS + 5))
ORDER = ((1, 0), (1, 1), (2, 0), (1, 2), (2, 1), (1, 3), (2, 2), (2, 3))
M1 = (0, 1, 3, 5)

EA_PAD, EB_PAD, EC_PAD = WA - 1, PB, WC - 1
EA_W, EB_W, EC_W = T + 2 * EA_PAD, T + 2 * EB_PAD, T + 2 * EC_PAD

VECTORS = [("norm_mix_g", LAYERS * KD), ("norm_ffn_g", LAYERS * KD), ("b_ada", LAYERS * 6 * KD), ("db_a", KA),
           ("ln_a_g", KA), ("ln_a_b", KA), ("pool_scale", KA), ("final_g", KD), ("dw_a", KA * WA),
           ("dw_c", KD * WC), ("c", KD * 2)]
VEC_AT = {}
VEC_N = 0
for _name, _n in VECTORS:
    VEC_AT[_name] = (VEC_N, _n)
    VEC_N += _n


class Count:

    def __init__(self, n=0):
        self.n, self.turns = n, []

    def at(self, ahead=0):
        value = self.n + ahead
        for turn, per in self.turns:
            value = turn * per + value
        return value

    def over(self, by):
        value = self.n // by
        for turn, per in self.turns:
            value = turn * (per // by) + value
        return value


@contextmanager
def loop(eng, times, *steps):
    with eng.Fori(0, times) as turn:
        starts = [c.n for c, _ in steps]
        for c, per in steps:
            c.turns.append((turn, per))
        yield turn
        for (c, per), start in zip(steps, starts):
            c.turns.pop()
            assert c.n - start == per, (c.n - start, per)
            c.n = start + per * times


class Walk:

    def __init__(self):
        self.use, self.act, self.dve = Count(), Count(), Count()

    def take(self, reader, n=1):
        self.use.n += n
        (self.act if reader == "act" else self.dve).n += n
        return self.use.n - 1

    def steps(self, act=0, dve=0):
        return (self.use, act + dve), (self.act, act), (self.dve, dve)


def _schedule():
    use = act = 0
    per_slot = [8 * (s // 4) + M1[s % 4] + 1 for s in range(ADA_SLOTS)]
    ada, w_in, residual, gate_act, gates_use, gates_act, expert_end = [], [], [], [], [], [], []
    for l in range(LAYERS):
        use += 1
        if l == 0:
            ada += [use + n for n in per_slot]
            use += 2 * ADA_SLOTS
            act += 2 * ADA_SLOTS
        w_in.append([use + 4 * (s + 1) for s in range(IN_SLOTS[l])])
        use += 4 * IN_SLOTS[l]
        act += (12, 16)[l]
        if l == 0:
            ada += [use + KA + n for n in per_slot]
            use += KA + 2 * ADA_SLOTS + 2
            act += KA + 2 * ADA_SLOTS
        use += 4 * OUT_SLOTS
        residual.append(use - act)
        use += 1
        use += NQ
        act += NQ
        gate_act.append(act)
        use += TILES * 12 + (T // STEP) * 4
        act += TILES * 10 + (T // STEP) * 4
        gates_use.append(use)
        gates_act.append(act)
        use += 8
        act += 8
        use += 8 * AHEAD + 12 * (GROUPS - AHEAD)
        act += 4 * (GROUPS - AHEAD)
        expert_end.append(use)
    return ada, w_in, residual, gate_act, gates_use, gates_act, expert_end


ADA_USED, IN_USED, RESIDUAL, GATE_ACT, GATES_USE, GATES_ACT, EXPERT_END = _schedule()
TILE_LINKS = 17


def build(nc, xT, vectors, state_a, state_b, state_c, w_pool, keys, whole_w, split_w, U, V,
          out_y, out_ap, out_as, out_bp, out_bs, out_cp, out_cs, gates_dram, act_dram, x_dram):
    with ExitStack() as ctx:
        def sb(name, shape, dt=F32):
            return ctx.enter_context(nc.sbuf_tensor(name, shape, dt))

        def sem(name):
            return ctx.enter_context(nc.semaphore(name))

        X = sb("X", [P, KD, T])
        H = sb("H", [P, KD, T])
        ACCF = sb("ACC", [P, KD * T])
        ACC = ACCF[:, :].rearrange("p (k t) -> p k t", k=KD)
        Z = ACC
        ring = sb("ring", [P, RING, SLOT])
        keyT = sb("keyT", [P, NQ, NKEYS])
        vec = sb("vec", [P, VEC_N])
        wpool = sb("wpool", [P, KA, P])
        ones = sb("ones", [P, P])
        ident = sb("ident", [P, P])
        iota = sb("iota", [P, P])
        inv_count = sb("inv_count", [P, PB + 1])
        mod = sb("mod", [P, LAYERS, 6 * KD, 2])
        scale = sb("scale", [P, LAYERS, 2, KD, 2])
        cact = sb("cact", [P, KD, 2])
        stat = sb("stat", [P, 3, T])
        carrier = sb("carrier", [P, 4])
        arena = sb("arena", [P, 18176])

        def part(at, *shape, dt=F32):
            n = int(np.prod(shape))
            assert at + n <= 18176, at + n
            v = arena[:, at:at + n]
            if dt is not F32:
                v = v.bitcast(dt)
            names = "abcd"[:len(shape)]
            if len(shape) > 1:
                sizes = {k: s for k, s in zip(names, shape)}
                v = v.rearrange(f"p ({' '.join(names)}) -> p {' '.join(names)}", **sizes)
            return v

        def vecs(name):
            at, n = VEC_AT[name]
            return vec[:, at:at + n]

        mod_rows = stat[:, :, :].rearrange("p a t -> p (a t)")[0:2, 0:1024].rearrange("c (b n) -> c b n", b=2)
        EA = part(0, KA, EA_W)
        EB = part(2416, KA, EB_W)
        CONV = part(4712, KA, EB_W)
        YC = part(7008, KA, T)
        SQ = part(9184, KA, T)
        PL = part(11360, KA, T)
        SG = part(13536, 2, T)
        PT = part(14624, 2, EB_W)
        BG = part(0, KD, T)
        EC = part(4352, KD, EC_W)
        YO = part(8736, KD, EC_W)
        QT = part(0, NQ, T)
        CAND = part(8704, HEADS, TOPK * TOPK)
        ZAP = part(10752, HEADS, TOPK * TOPK)
        ZT = part(10752, NQ, NKEYS)
        PICK = part(8704, P, TOPK)
        PLACE = part(10752, 2, P, dt=U32)
        PLF = part(11008, 2, P)
        O1 = part(8704, 4, SUB, P)
        O2 = part(12800, 4, SUB, P)
        IT = part(16896, 2, P)
        GT = part(17152, P)
        small = stat[:, :, :].rearrange("p a t -> p (a t)")
        V16 = small[:, 0:256].rearrange("p (h j k) -> p h j k", h=HEADS, j=2)
        I16 = small[:, 256:512].bitcast(U32).rearrange("p (h j k) -> p h j k", h=HEADS, j=2)
        IF = small[:, 512:768].rearrange("p (h j k) -> p h j k", h=HEADS, j=2)
        C8 = small[:, 768:896].rearrange("p (h k) -> p h k", h=HEADS)
        ZS = small[:, 896:904]
        RZ = small[:, 904:912]
        GG = small[:, 912:1040].rearrange("p (h k) -> p h k", h=HEADS)
        P8 = small[:, 1040:1168].bitcast(U32).rearrange("p (h k) -> p h k", h=HEADS)
        KEYS = small[:, 1168:1424].rearrange("p (j n) -> p j n", j=2)
        stage = ACCF[:, 0:4096].rearrange("p (s g t e) -> p s g t e", s=2, g=BODIES, t=16)
        HM = [a.bitcast(F16).rearrange("p (s k t) -> p s k t", s=2, k=KD) for a in (ACCF[:, :], part(13120, KD * T))]
        H16 = X[:, :, :].rearrange("p k t -> p (k t)").bitcast(F16).rearrange("p (s k t) -> p s k t", s=2, k=KD)
        ahead = H[:, :, :].rearrange("p (a j) t -> p a j t", a=2)
        AB = part(0, 2, 4, T)
        GB = arena[:, 4352:4352 + 2 * T * 8]
        WT = part(13056, 2 * 4 * T).bitcast(F16).rearrange("p (g s j t) -> p g s j t", g=2, s=2, j=4)
        AG = stat[:, 0:2, :]
        raw = [ring[:, i, :] for i in range(2)]
        parts = [ring[:, 2 + i, :].bitcast(F16).rearrange("p (s n) -> p s n", s=2) for i in range(2)]

        PS = ctx.enter_context(nc.psum_tensor("PS", [P, PAIRS, 1024], F32))

        vec_in, x_in, state_in, pool_in, keys_in = (sem(x) for x in "vec_in x_in state_in pool_in keys_in".split())
        slot_in = [sem(f"slot_in{i}") for i in range(RING)]
        mm_done = sem("mm_done")
        act_read = sem("act_read")
        dve_read = sem("dve_read")
        consts_made, pads_made, c_in = sem("consts_made"), sem("pads_made"), sem("c_in")
        c_sigmoid, cact_ready, mod_ready = sem("c_sigmoid"), sem("cact_ready"), sem("mod_ready")
        x_ready, sq_ready, std_ready, xn_ready, h_ready = (sem(x) for x in "x_ready sq_ready std_ready xn_ready h_ready".split())
        glu_ready, pooled, conv_ready, centered, ln_sig, z_ready = (
            sem(x) for x in "glu_ready pooled conv_ready centered ln_sig z_ready".split())
        shifted, exped, gates_ready = sem("shifted"), sem("exped"), sem("gates_ready")
        o1_ready, o2_ready, weighted, keys_found = (sem(x) for x in "o1_ready o2_ready weighted keys_found".split())
        g_written = [sem(f"g_written{i}") for i in range(2)]
        raw_in = [sem(f"raw_in{i}") for i in range(2)]
        high_made = [sem(f"high_made{i}") for i in range(2)]
        split = [sem(f"split{i}") for i in range(2)]
        act_stored = [sem(f"act_stored{i}") for i in range(2)]
        act_in = [sem(f"act_in{i}") for i in range(2)]
        x_stored, x_back = sem("x_stored"), sem("x_back")
        scaled = sem("scaled")
        hm_high, hm_split = sem("hm_high"), sem("hm_split")
        h_high, h_split, wf_ready, w_high = sem("h_high"), sem("h_split"), sem("wf_ready"), sem("w_high")
        g_in, w_ready, acc_zero = sem("g_in"), sem("w_ready"), sem("acc_zero")
        dve_step, pool_step, y_ready, y_out, state_out = (sem(x) for x in "dve_step pool_step y_ready y_out state_out".split())

        SEG = ((0, NP_, 0), (NP_, T, 1))
        mod_at = {"sh1": 0, "sc1": 1, "g1": 2, "sh2": 3, "sc2": 4, "g2": 5}
        CONSTS = 5
        NORM = (0, KD + KA, 2 * KD + KA, 3 * KD + KA, 4 * KD + KA)
        STEPS = T // STEP
        PASSES = ((0, 0), (0, 1), (1, 0))

        def ps(u, n=T):
            return PS[:, u % PAIRS, 0:n]

        def ps_halves(u):
            return PS[:, u % PAIRS, :].rearrange("p (b c) -> p b c", b=2)[:, :, 0:HALF]

        block = ctx.enter_context(nc.Block())

        @block.sync
        def _(sp):
            def load_whole(f, semaphore, n):
                if n is not None:
                    sp.wait_ge(semaphore, n)
                sp.dma_start(ring[:, f % RING, :], whole_w[f if f < LAYERS * ADA_SLOTS else f - 2 * (1 + (f > 28))]).then_inc(
                    slot_in[f % RING], 16)

            def load_raw(lane, src, n):
                if n is not None:
                    sp.wait_ge(split[lane], n)
                sp.dma_start(raw[lane], src).then_inc(raw_in[lane], 16)

            def group_of(source, l, group):
                return source[l, group] if isinstance(group, int) else \
                    source[l, bass.ds(group, 1)].rearrange("o p n -> (o p) n")

            sp.dma_start(vec[:, :], vectors).then_inc(vec_in, 16)
            sp.dma_start(X[:, :, :], xT).then_inc(x_in, 16)
            view = gates_dram.rearrange("p g t e -> g p (t e)")
            for s in range(2):
                sp.sem_inc(g_written[s], 16)
                sp.sem_inc(act_stored[s], 16)
            for l in range(LAYERS):
                if l == 0:
                    for f in range(ADA_SLOTS):
                        load_whole(f, mm_done, ADA_USED[f - RING] if f >= RING else None)
                    sp.wait_ge(mm_done, ADA_USED[ADA_SLOTS - 3])
                    load_raw(1, split_w[0], None)
                    load_raw(0, split_w[1], None)
                    load_raw(1, split_w[2], 1)
                    for f in range(ADA_SLOTS, 2 * ADA_SLOTS):
                        n = f - ADA_SLOTS
                        if n < 2:
                            load_whole(f, split[n], 1 + n)
                        elif n < 4:
                            load_whole(f, mm_done, IN_USED[0][n - 1])
                        else:
                            load_whole(f, mm_done, ADA_USED[f - RING])
                    for f in (26, 27):
                        load_whole(f, mm_done, ADA_USED[f - RING])
                    sp.wait_ge(mm_done, ADA_USED[2 * ADA_SLOTS - 3])
                    for lane in range(2):
                        load_raw(lane, split_w[3 + lane], None)
                    q_slot = 5
                else:
                    for i in range(IN_SLOTS[1] + 2):
                        load_raw(i % 2, split_w[7 + i], BEFORE[0][i % 2] + GROUPS + i // 2)
                    for f in (30, 31):
                        load_whole(f, mm_done, IN_USED[1][f - 26])
                    q_slot = 7 + IN_SLOTS[1] + 2
                sp.dma_start(keyT[:, :, :], keys[l]).then_inc(keys_in, 16)
                sp.wait_ge(dve_read, RESIDUAL[l])
                sp.dma_start(x_dram, X[:, :, :].rearrange("p k t -> p (k t)")).then_inc(x_stored, 16)
                for lane in range(2):
                    load_raw(lane, split_w[q_slot + lane], BEFORE[l][lane] - 1)
                for lane in range(2):
                    load_raw(lane, U[l, lane], BEFORE[l][lane])

                def gate_tile(tile, n_steps):
                    last_tile = isinstance(tile, int)
                    for lane in range(2):
                        load_raw(lane, group_of(U, l, tile * 2 + (2 + lane)), tile + (BEFORE[l][lane] + 1))
                    for lane in range(2):
                        sp.wait_ge(act_read, tile * 26 + (GATE_ACT[l] + 4 * lane + 4))
                        at = tile * 2 + lane
                        dst = act_dram[:, at, :] if last_tile else act_dram[:, bass.ds(at, 1), :].rearrange("p o n -> p (o n)")
                        sp.dma_start(dst, ahead[:, lane, :, :].rearrange("p j t -> p (j t)")).then_inc(act_stored[lane], 16)
                    if last_tile:
                        spill(tile, 0)
                    else:
                        with sp.Fori(0, n_steps) as step:
                            spill(tile, step)

                def spill(tile, step):
                    for s in range(2):
                        sp.wait_ge(act_read, tile * 26 + step * 4 + (GATE_ACT[l] + 10 + 2 * s + 2))
                        sp.dma_start(gates_dram[:, :, bass.ds(tile * P + step * STEP + 16 * s, 16), :],
                                     stage[:, s, :, :, :]).then_inc(g_written[s], 16)

                with sp.Fori(0, TILES - 1) as tile:
                    gate_tile(tile, P // STEP)
                gate_tile(TILES - 1, 1)
                for s in range(2):
                    sp.wait_ge(g_written[s], 16 * ((l + 1) * STEPS + 1))
                    sp.wait_ge(act_stored[s], 16 * (l * (TILES + 1) + TILES + 1))
                sp.wait_ge(mm_done, GATES_USE[l])
                sp.wait_ge(act_read, GATES_ACT[l])
                for k in range(2):
                    if k:
                        sp.wait_ge(g_in, 16 * (l * BODIES + k))
                    sp.dma_start(GB[:, k * T * 8:(k + 1) * T * 8], view[k]).then_inc(g_in, 16)
                    sp.dma_start(AB[:, k, :, :].rearrange("p j t -> p (j t)"), act_dram[:, k, :]).then_inc(act_in[k], 16)

                for lane in range(2):
                    load_raw(lane, V[l, lane], BEFORE[l][lane] + AHEAD // 2)
                    sp.wait_ge(act_read, GATES_ACT[l] + 4 * lane + 4)
                    sp.dma_start(act_dram[:, 2 * TILES + lane, :],
                                 ahead[:, lane, :, :].rearrange("p j t -> p (j t)")).then_inc(act_stored[lane], 16)

                def next_g(body):
                    sp.wait_ge(w_ready, body * 8 + (l * NKEYS + 10))
                    sp.wait_ge(g_in, body * 16 + 16 * (l * BODIES + 2))
                    if isinstance(body, int):
                        dst, src = GB[:, (body % 2) * T * 8:(body % 2 + 1) * T * 8], view[body + 2]
                    else:
                        dst = GB[:, bass.ds((body % 2) * (T * 8), T * 8)]
                        src = view[bass.ds(body + 2, 1)].rearrange("o p n -> (o p) n")
                    sp.dma_start(dst, src).then_inc(g_in, 16)

                for lane in range(2):
                    sp.wait_ge(act_stored[lane], 16 * ((l + 1) * (TILES + 1) + 1))
                with sp.Fori(0, AHEAD // 2 - 1) as body:
                    for lane in range(2):
                        group = body * 2 + (2 + lane)
                        load_raw(lane, group_of(V, l, group), body + (BEFORE[l][lane] + AHEAD // 2 + 1))
                        sp.wait_ge(w_ready, body * 8 + (l * NKEYS + 4 * lane + 4 + 2))
                        sp.dma_start(AB[:, lane, :, :].rearrange("p j t -> p (j t)"),
                                     act_dram[:, bass.ds(group, 1), :].rearrange("p o n -> p (o n)")).then_inc(act_in[lane], 16)
                    next_g(body)
                for lane in range(2):
                    load_raw(lane, group_of((U, V)[lane], l, AHEAD), BEFORE[l][lane] + AHEAD)
                next_g(AHEAD // 2 - 1)

                def groups(body, n):
                    for k in range(n):
                        for lane in range(2):
                            load_raw(lane, group_of((U, V)[lane], l, body * 2 + (k + 1)), body * 2 + (BEFORE[l][lane] + k + 1))

                with sp.Fori(AHEAD // 2, BODIES - 2) as body:
                    groups(body, 2)
                    next_g(body)
                groups(BODIES - 2, 2)
                groups(BODIES - 1, 1)
                sp.wait_ge(mm_done, EXPERT_END[l] - KD)
                sp.dma_start(X[:, :, :].rearrange("p k t -> p (k t)"), x_dram).then_inc(x_back, 16)
            for k in range(KD):
                sp.wait_ge(y_ready, k + 1)
                sp.dma_start(out_y[:, k, :], H[:, k, :]).then_inc(y_out, 16)
            sp.wait_ge(y_out, 16 * KD)
            sp.wait_ge(state_out, 16 * 6)

        @block.tensor
        def _(pe):
            w, slot, wts, sub, lanes = Walk(), Count(), Count(2), Count(), (Count(), Count())
            last = [None] * PAIRS

            def begin(reader):
                pair = w.use.n % PAIRS
                if last[pair] is not None:
                    who, value = last[pair]
                    pe.wait_ge(act_read if who == "act" else dve_read, value)
                u = w.take(reader)
                last[pair] = (reader, (w.act if reader == "act" else w.dve).at())
                return u

            def drained():
                for who, count in ((act_read, w.act), (dve_read, w.dve)):
                    if count.n:
                        pe.wait_ge(who, count.at())

            def from_turn_before(reader):
                count = w.act if reader == "act" else w.dve
                for i in range(PAIRS):
                    last[(w.use.n + i) % PAIRS] = (reader, count.at(i - PAIRS + 1))

            def slot_ready():
                pe.wait_ge(slot_in[slot.n % RING], slot.over(RING) * 16 + 16)
                slot.n += 1
                return ring[:, (slot.n - 1) % RING, :]

            def project(slots, src, readers, ready):
                slot.n += 2
                for s in range(slots):
                    wt = slot_ready()
                    for m in range(4):
                        u = begin(readers[4 * s + m])
                        for k in range(KD):
                            if s == 0 and m == 0:
                                ready(k)
                            for a, b, _ in SEG:
                                mm = pe.matmul(ps(u)[:, a:b], wt[:, k * 512 + m * P:k * 512 + (m + 1) * P], src[:, k, a:b],
                                               start=(k == 0), stop=(k == KD - 1))
                        mm.then_inc(mm_done, 1)

            def project_parts(slots, src, reader_of, ready):
                for s in range(slots):
                    lane = (s + (slots == IN_SLOTS[0])) % 2
                    lanes[lane].n += 1
                    pe.wait_ge(split[lane], lanes[lane].at())
                    for m in range(4):
                        u = begin(reader_of(4 * s + m))
                        for k in range(KD):
                            if s == 0 and m == 0:
                                ready(k)
                            for n, (pw, ph) in enumerate(PASSES):
                                for a, b, _ in SEG:
                                    mm = pe.matmul(ps(u)[:, a:b], parts[lane][:, pw, k * 512 + m * P:k * 512 + (m + 1) * P],
                                                   src[:, ph, k, a:b], start=(k == n == 0), stop=(k == KD - 1 and n == 2))
                        mm.then_inc(mm_done, 1)

            def column_sums(src, chunks, semaphore, value, gap=0):
                u = begin("dve")
                for k in range(chunks):
                    pe.wait_ge(semaphore, value + k)
                    for a, b, s in SEG:
                        mm = pe.matmul(ps(u)[:, a:b], ones[:, :], src[:, k, a + s * gap:b + s * gap],
                                       start=(k == 0), stop=(k == chunks - 1))
                mm.then_inc(mm_done, 1)

            def ada_slots():
                copied = {}
                for which, s in ORDER:
                    if which == 1:
                        wt = slot_ready()
                        u = begin("act")
                        copied[s] = w.act.at()
                        for k in range(KD):
                            mm = pe.matmul(PS[0:2, u % PAIRS, 0:512], cact[:, k, :], wt[:, k * 512:(k + 1) * 512],
                                           start=(k == 0), stop=(k == KD - 1))
                    else:
                        u = begin("act")
                        pe.wait_ge(act_read, copied[s])
                        for m in range(4):
                            mm = pe.matmul(ps(u)[:, 2 * m:2 * m + 2], mod_rows[:, s % 2, m * P:(m + 1) * P], ident[0:2, 0:2],
                                           start=True, stop=True)
                    mm.then_inc(mm_done, 1)

            def ada(turns):
                drained()
                with loop(pe, turns, *w.steps(act=8), (slot, 4)):
                    from_turn_before("act")
                    ada_slots()
                from_turn_before("act")

            def u_group(lane):
                pe.wait_ge(split[lane], lanes[lane].at(1))
                for j in range(4):
                    u = begin("act")
                    for k in range(KD):
                        for n, (pu, ph) in enumerate(PASSES):
                            for half in range(2):
                                mm = pe.matmul(ps_halves(u)[:, half, :], parts[lane][:, pu, k * 512 + j * P:k * 512 + (j + 1) * P],
                                               H16[:, ph, k, half * HALF:(half + 1) * HALF],
                                               start=(k == n == 0), stop=(k == KD - 1 and n == 2))
                    mm.then_inc(mm_done, 1)
                lanes[lane].n += 1

            def v_group(lane, grp):
                pe.wait_ge(split[lane], lanes[lane].at(1))
                for c in range(KD):
                    u = begin("dve")
                    for j in range(4):
                        if c == 0:
                            pe.wait_ge(w_ready, wts.at(j + 1))
                        for n, (pv, pw) in enumerate(PASSES):
                            for half in range(2):
                                mm = pe.matmul(ps_halves(u)[:, half, :], parts[lane][:, pv, j * D + c * P:j * D + (c + 1) * P],
                                               WT[:, grp, pw, j, half * HALF:(half + 1) * HALF],
                                               start=(j == n == 0), stop=(j == 3 and n == 2))
                    mm.then_inc(mm_done, 1)
                wts.n += 4
                lanes[lane].n += 1

            pe.wait_ge(consts_made, CONSTS)
            pe.wait_ge(cact_ready, 1)
            for l in range(LAYERS):
                column_sums(H, KD, sq_ready, NORM[2 * l] + 1)
                if l == 0:
                    ada_slots()
                    ada(ADA_SLOTS // 4 - 1)
                project_parts(IN_SLOTS[l], HM[l], lambda m: "act" if m < 16 else "dve",
                              lambda k: pe.wait_ge(hm_split, KD * l + k + 1))
                if l == 0:
                    pe.wait_ge(pool_in, 16)
                    for g in range(KA):
                        pe.wait_ge(pooled, g + 1)
                        u = begin("act")
                        for a, b, _ in SEG:
                            mm = pe.matmul(ps(u)[:, a:b], wpool[:, g, :], PL[:, g, a:b], start=True, stop=True)
                        mm.then_inc(mm_done, 1)
                    branch = w.act.at()
                    ada(ADA_SLOTS // 4)
                    column_sums(CONV, KA, conv_ready, 1, EA_PAD)
                    column_sums(SQ, KA, sq_ready, KD + 1)
                    project(OUT_SLOTS, Z, ["dve"] * 8,
                            lambda k: pe.wait_ge(z_ready, k + 1) if k < KA else pe.wait_ge(act_read, branch))
                else:
                    project(OUT_SLOTS, Z, ["dve"] * 8, lambda k: pe.wait_ge(z_ready, KA + k + 1))
                column_sums(H, KD, sq_ready, NORM[2 * l + 1] + 1)
                project_parts(Q_SLOTS, H16, lambda m: "act", lambda k: pe.wait_ge(h_split, KD * l + k + 1))

                pe.wait_ge(keys_in, 16 * (l + 1))
                pe.wait_ge(act_read, w.act.at())
                for t in range(5):
                    n = P if t < 4 else NS_
                    for j in range(2):
                        u = begin("dve")
                        for q in range(8):
                            mm = pe.matmul(PS[0:n, u % PAIRS, q * P:(q + 1) * P], QT[:, 8 * j + q, t * P:t * P + n],
                                           keyT[:, 8 * j + q, :], start=True, stop=True)
                        mm.then_inc(mm_done, 1)
                    for lane in range(2):
                        u_group(lane)
                    pe.wait_ge(keys_found, l * 5 + t + 1)
                    u = begin("act")
                    for j in range(2):
                        mm = pe.transpose(ps(u)[:, j * P:(j + 1) * P], KEYS[:, j, :], ident[:, :])
                    mm.then_inc(mm_done, 1)
                    pe.wait_ge(gates_ready, l * 5 + t + 1)
                    u = begin("act")
                    pe.transpose(ps(u, P), GG.rearrange("p h k -> p (h k)"), ident[:, :]).then_inc(mm_done, 1)
                    drained()
                    with loop(pe, 4 if t < 4 else 1, *w.steps(act=4), (sub, 4)):
                        from_turn_before("act")
                        for s in range(4):
                            u = begin("act")
                            pe.wait_ge(o1_ready, sub.at(s + 1))
                            pe.wait_ge(weighted, sub.at(s + 1))
                            for i in range(SUB):
                                mm = pe.matmul(ps(u, 1024)[:, i * P:(i + 1) * P], O2[:, s, i, :], O1[:, s, i, :],
                                               start=True, stop=True)
                            mm.then_inc(mm_done, 1)
                        sub.n += 4
                    from_turn_before("act")

                for lane in range(2):
                    u_group(lane)
                drained()
                with loop(pe, AHEAD // 2, *w.steps(dve=16), (lanes[0], 1), (lanes[1], 1), (wts, 8)):
                    from_turn_before("dve")
                    for grp in range(2):
                        v_group(grp, grp)
                drained()
                with loop(pe, BODIES - AHEAD // 2, *w.steps(act=8, dve=16), (lanes[0], 2), (lanes[1], 2), (wts, 8)):
                    from_turn_before("dve")
                    for grp in range(2):
                        u_group(0)
                        v_group(1, grp)
                from_turn_before("dve")
            column_sums(H, KD, sq_ready, NORM[4] + 1)

        @block.scalar
        def _(act):
            w, body, wts, lanes, scalings = Walk(), Count(1), Count(2), (Count(), Count()), Count()

            def next_use():
                act.wait_ge(mm_done, w.use.at(1))
                return w.take("act")

            def squares(src, dst, chunks, semaphore, value):
                for k in range(chunks):
                    act.wait_ge(semaphore, value + k)
                    act.activation(dst[:, k, :], src[:, k, :], ACT.Square).then_inc(sq_ready, 1)

            def root():
                w.take("dve")
                act.wait_ge(dve_read, w.dve.at())
                act.activation(stat[:, 1, :], stat[:, 0, :], ACT.Sqrt).then_inc(std_ready, 1)

            def modulate(l, which):
                sh = mod_at["sh1" if which == 0 else "sh2"] * KD
                for k in range(KD):
                    act.wait_ge(xn_ready, NORM[2 * l + which] + k + 1)
                    for a, b, s in SEG:
                        ins = act.activation(H[:, k, a:b], H[:, k, a:b], ACT.Identity,
                                             scale=scale[:, l, which, k, s:s + 1], bias=mod[:, l, sh + k, s:s + 1])
                    ins.then_inc(h_ready, 1)

            def high(lane, scale):
                lanes[lane].n += 1
                act.wait_ge(raw_in[lane], lanes[lane].at() * 16)
                act.wait_ge(mm_done, w.use.at())
                act.activation(parts[lane][:, 0, :], raw[lane], ACT.Copy, scale=scale).then_inc(high_made[lane], 1)

            def scale_and_high(lane):
                lanes[lane].n += 1
                scalings.n += 1
                act.wait_ge(raw_in[lane], lanes[lane].at() * 16)
                act.activation(raw[lane], raw[lane], ACT.Copy, scale=U_SCALE).then_inc(scaled, 1)
                act.wait_ge(scaled, scalings.at())
                act.wait_ge(mm_done, w.use.at())
                act.copy(parts[lane][:, 0, :], raw[lane]).then_inc(high_made[lane], 1)

            def high_part(src, dst, semaphore, value, signal):
                for k in range(KD):
                    act.wait_ge(semaphore, value + k)
                    act.copy(dst[:, 0, k, :], src[:, k, :]).then_inc(signal, 1)

            def store_state(dst, src):
                act.dma_start(dst, src).then_inc(state_out, 16)

            act.dma_start(EA[:, :, EA_PAD + NP_:2 * EA_PAD + NP_], state_a).then_inc(state_in, 16)
            act.dma_start(EB[:, :, EB_PAD + NP_:2 * EB_PAD + NP_], state_b).then_inc(state_in, 16)
            act.dma_start(wpool[:, :, :], w_pool).then_inc(pool_in, 16)
            act.wait_ge(vec_in, 16)
            act.activation(cact[:, :, :].rearrange("p k s -> p (k s)"), vecs("c"), ACT.Sigmoid).then_inc(c_sigmoid, 1)

            def ada(l):
                with loop(act, ADA_SLOTS // 4, *w.steps(act=8)) as turn:
                    for which, s in ORDER:
                        u = next_use()
                        if which == 1:
                            act.copy(mod_rows[:, s % 2, :], PS[0:2, u % PAIRS, 0:512]).then_inc(act_read, 1)
                        else:
                            act.copy(mod[:, l, bass.ds(turn * 16 + 4 * s, 4), :],
                                     ps(u, 8).rearrange("p (m s) -> p m s", s=2)).then_inc(act_read, 1)

            for l in range(LAYERS):
                if l == 0:
                    act.wait_ge(x_in, 16)
                    for k in range(KD):
                        act.activation(H[:, k, :], X[:, k, :], ACT.Square).then_inc(sq_ready, 1)
                    root()
                    act.wait_ge(xn_ready, 1)
                    ada(0)
                else:
                    squares(X, H, KD, x_ready, 1)
                for lane in ((1, 0), (0, 1))[l]:
                    high(lane, U_SCALE)
                if l > 0:
                    root()
                act.wait_ge(mod_ready, l + 1)
                modulate(l, 0)
                high_part(H, HM[l], h_ready, 2 * KD * l + 1, hm_high)
                if l == 0:
                    act.wait_ge(consts_made, CONSTS)
                    for c in range(KA):
                        u = next_use()
                        for a, b, s in SEG:
                            ins = act.activation(EA[:, c, a + EA_PAD * (1 + s):b + EA_PAD * (1 + s)], ps(u)[:, a:b], ACT.Copy,
                                                 scale=1.0 / U_SCALE)
                        ins.then_inc(act_read, 1)
                    high(1, U_SCALE)
                    for c in range(KA):
                        u = next_use()
                        if c >= 2:
                            act.wait_ge(glu_ready, c - 1)
                        act.activation(SG[:, c % 2, :], ps(u), ACT.Sigmoid, scale=1.0 / U_SCALE).then_inc(act_read, 1)
                    for c in range(KA):
                        u = next_use()
                        for a, b, s in SEG:
                            ins = act.activation(EB[:, c, a + EB_PAD * (1 + s):b + EB_PAD * (1 + s)], ps(u)[:, a:b], ACT.Copy,
                                                 scale=1.0 / U_SCALE)
                        ins.then_inc(act_read, 1)
                    act.wait_ge(glu_ready, KA)
                    store_state(out_ap, EA[:, :, NP_:NP_ + EA_PAD])
                    store_state(out_as, EA[:, :, EA_W - EA_PAD:EA_W])
                    act.wait_ge(act_read, w.act.at())
                    store_state(out_bp, EB[:, :, NP_:NP_ + EB_PAD])
                    store_state(out_bs, EB[:, :, EB_W - EB_PAD:EB_W])
                    for g in range(KA):
                        u = next_use()
                        act.activation(Z[:, KA + g, :], ps(u), ACT.Identity,
                                       scale=vecs("pool_scale")[:, g:g + 1]).then_inc(act_read, 1)
                    ada(1)
                    w.take("dve")
                    squares(YC, SQ, KA, centered, 1)
                    root()
                    for k in range(KA):
                        act.wait_ge(xn_ready, KD + k + 1)
                        act.activation(SQ[:, k, :], YC[:, k, :], ACT.Sigmoid, scale=vecs("ln_a_g")[:, k:k + 1],
                                       bias=vecs("ln_a_b")[:, k:k + 1]).then_inc(ln_sig, 1)
                else:
                    act.wait_ge(x_ready, KD)
                    act.wait_ge(pads_made, 1)
                    act.wait_ge(c_in, 16)
                    for c in range(2 * KD):
                        u = next_use()
                        if c < KD:
                            act.activation(BG[:, c, :], ps(u), ACT.Copy, scale=1.0 / U_SCALE).then_inc(act_read, 1)
                        else:
                            for a, b, s in SEG:
                                ins = act.activation(EC[:, c - KD, a + EC_PAD * (1 + s):b + EC_PAD * (1 + s)], ps(u)[:, a:b],
                                                     ACT.Copy, scale=1.0 / (U_SCALE * U_SCALE))
                            ins.then_inc(act_read, 1)
                        if c % 4 == 3:
                            high(c // 4 % 2, U_SCALE)
                    w.take("dve", KD)
                    act.wait_ge(dve_read, w.dve.at())
                    store_state(out_cp, EC[:, :, NP_:NP_ + EC_PAD])
                    store_state(out_cs, EC[:, :, EC_W - EC_PAD:EC_W])
                w.take("dve", KD)
                squares(X, H, KD, dve_read, w.dve.at(1 - KD))
                high(0, U_SCALE)
                root()
                high(1, U_SCALE)
                modulate(l, 1)
                act.wait_ge(x_stored, 16 * (l + 1))
                high_part(H, H16, h_ready, 2 * KD * l + KD + 1, h_high)
                act.wait_ge(state_out, (64, 96)[l])
                for c in range(NQ):
                    u = next_use()
                    act.activation(QT[:, c, :], ps(u), ACT.Copy, scale=1.0 / U_SCALE).then_inc(act_read, 1)
                    if c in (3, 7):
                        high(c // 4, U_SCALE)
                    if c in (11, 15):
                        scale_and_high(c // 4 - 2)

                def gelu(dst):
                    u = next_use()
                    act.activation(dst.rearrange("p (b c) -> p b c", b=2), ps_halves(u), ACT.Gelu_apprx_tanh,
                                   scale=1.0 / U_SCALE).then_inc(act_read, 1)

                def tile_and_steps(t, steps):
                    w.take("dve", 2)
                    act.wait_ge(act_stored[0], t * 16 + 16 * (l + 1))
                    for j in range(4):
                        gelu(ahead[:, 0, j, :])
                    scale_and_high(0)
                    act.wait_ge(act_stored[1], t * 16 + 16 * (l + 1))
                    for j in range(4):
                        if j == 2:
                            act.wait_ge(shifted, t + 1)
                            act.activation(GG, GG, ACT.Exp).then_inc(exped, 1)
                        gelu(ahead[:, 1, j, :])
                    u = next_use()
                    act.copy(IT.rearrange("p j t -> p (j t)"), ps(u, 2 * P)).then_inc(act_read, 1)
                    u = next_use()
                    act.copy(GT, ps(u, P)).then_inc(act_read, 1)
                    scale_and_high(1)
                    with loop(act, steps, *w.steps(act=4), (body, 1)):
                        for s in range(4):
                            if s % 2 == 0:
                                act.wait_ge(g_written[s // 2], body.at() * 16)
                            u = next_use()
                            dst = stage[:, s // 2, :, SUB * (s % 2):SUB * (s % 2) + SUB, :]
                            act.copy(dst, ps(u, 1024).rearrange("p (t g e) -> p g t e", t=SUB, e=8)).then_inc(act_read, 1)
                        body.n += 1

                with loop(act, TILES - 1, (w.use, 28), (w.act, 26), (w.dve, 2), (body, 4),
                          (lanes[0], 1), (lanes[1], 1), (scalings, 2)) as turn:
                    tile_and_steps(turn + TILES * l, 4)
                tile_and_steps(TILES * l + TILES - 1, 1)

                for lane in range(2):
                    act.wait_ge(act_stored[lane], 16 * (l * (TILES + 1) + TILES + 1))
                    for j in range(4):
                        gelu(ahead[:, lane, j, :])
                    if lane == 0:
                        high(0, 1.0)
                with loop(act, AHEAD // 2 - 1, *w.steps(dve=16), (lanes[0], 1), (lanes[1], 1)):
                    for lane in (1, 0):
                        high(lane, 1.0)
                        w.take("dve", KD)
                high(1, 1.0)
                w.take("dve", KD)
                high(0, U_SCALE)
                w.take("dve", KD)
                wts.n += 4 * AHEAD

                def expert_body(groups_ahead):
                    for grp in range(2):
                        high(1, 1.0)
                        for j in range(4):
                            act.wait_ge(w_ready, wts.at(j - 1))
                            gelu(AG[:, j % 2, :])
                        wts.n += 4
                        if grp < groups_ahead:
                            high(0, U_SCALE)
                        w.take("dve", KD)

                with loop(act, BODIES - AHEAD // 2 - 1, *w.steps(act=8, dve=16), (wts, 8), (lanes[0], 2), (lanes[1], 2)):
                    expert_body(2)
                expert_body(1)
            act.wait_ge(x_back, 16 * LAYERS)
            squares(X, H, KD, x_ready, KD + 1)
            root()

        @block.gpsimd
        def _(pool):
            w, sub, lanes = Walk(), Count(), (Count(), Count())
            steps = 0

            def link(ins):
                nonlocal steps
                steps += 1
                ins.then_inc(pool_step, 1)
                pool.wait_ge(pool_step, steps)

            pool.memset(ones[:, :], 1.0).then_inc(consts_made, 1)
            link(pool.memset(ident[:, :], 0.0))
            pool.affine_select(out=ident[:, :], in_=ident[:, :], compare_op=ALU.not_equal, fill=1.0, base=0,
                               pattern=[[-1, P]], channel_multiplier=1).then_inc(consts_made, 1)
            pool.iota(iota[:, :], [[1, P]], base=0, channel_multiplier=0,
                      allow_small_or_imprecise_dtypes=True).then_inc(consts_made, 1)
            for i in range(PB + 1):
                ins = pool.memset(inv_count[:, i:i + 1], 1.0 / (i + 1))
            link(ins)
            pool.memset(EA[:, :, 0:EA_PAD], 0.0).then_inc(consts_made, 1)
            pool.memset(EB[:, :, 0:EB_PAD], 0.0).then_inc(consts_made, 1)
            for l in range(LAYERS):
                w.take("dve")
                if l == 0:
                    w.take("act", 2 * ADA_SLOTS)
                    pool.wait_ge(state_in, 32)
                    pool.wait_ge(consts_made, CONSTS)
                    w.take("act", 2 * KA)
                    for g, wnd in enumerate(WINDOWS):
                        w.take("act")
                        pool.wait_ge(act_read, w.act.at())
                        src, have = EB[:, g, :], 1
                        for i in range(g + 1):
                            dst = PT[:, i % 2, :]
                            link(pool.tensor_tensor(dst[:, 2 * have - 1:EB_W], src[:, 2 * have - 1:EB_W],
                                                    src[:, have - 1:EB_W - have], ALU.add))
                            src, have = dst, 2 * have
                        for a, b, s in SEG:
                            o = EB_PAD * (1 + s)
                            link(pool.tensor_scalar(PL[:, g, a:b], src[:, a + o:b + o], 1.0 / wnd, None, ALU.mult))
                        link(pool.tensor_tensor(PL[:, g, 0:wnd], src[:, EB_PAD:EB_PAD + wnd], inv_count[:, 0:wnd], ALU.mult))
                        for a, b, s in SEG:
                            o = EB_PAD * (1 + s)
                            ins = pool.tensor_tensor(PL[:, g, a:b], PL[:, g, a:b], EB[:, g, a + o:b + o], ALU.subtract)
                        ins.then_inc(pooled, 1)
                    w.take("act", KA + 2 * ADA_SLOTS)
                    w.take("dve", 2)
                else:
                    pool.wait_ge(x_ready, KD)
                    pool.memset(EC[:, :, 0:EC_PAD], 0.0).then_inc(pads_made, 1)
                    pool.dma_start(EC[:, :, EC_PAD + NP_:2 * EC_PAD + NP_], state_c).then_inc(c_in, 16)
                    w.take("act", 2 * KD)
                    w.take("dve", KD)
                w.take("dve", KD + 1)
                w.take("act", NQ)

                def low(lane):
                    lanes[lane].n += 1
                    pool.wait_ge(high_made[lane], lanes[lane].at())
                    pool.tensor_tensor(parts[lane][:, 1, :], raw[lane], parts[lane][:, 0, :], ALU.subtract).then_inc(split[lane], 1)

                def tile_and_steps(steps):
                    low(1)
                    low(0)
                    w.take("dve", 2)
                    w.take("act", 10)
                    transposed = w.act.at()
                    with loop(pool, steps, *w.steps(act=4), (sub, 4)) as turn:
                        pool.wait_ge(act_read, transposed)
                        for s in range(4):
                            tok = bass.ds(turn * STEP + SUB * s, SUB)
                            pool.wait_ge(o2_ready, sub.at(s + 1))
                            pool.tensor_tensor(O2[:, s, :, :], O2[:, s, :, :],
                                               GT[:, tok].unsqueeze(2).to_broadcast([P, SUB, P]), ALU.mult).then_inc(weighted, 1)
                        w.take("act", 4)
                        sub.n += 4

                for lane in range(2):
                    lanes[lane].n = BEFORE[l][lane]
                low(0)
                with loop(pool, 4, (w.use, 28), (w.act, 26), (w.dve, 2), (sub, 16), (lanes[0], 1), (lanes[1], 1)):
                    tile_and_steps(4)
                tile_and_steps(1)
                low(1)
                for s in range(2):
                    pool.wait_ge(g_written[s], 16 * ((l + 1) * STEPS + 1))
                pool.memset(ACCF[:, :], 0.0).then_inc(acc_zero, 1)
                w.take("act", 8 + 4 * (GROUPS - AHEAD))
                w.take("dve", 8 * GROUPS)

        @block.vector
        def _(dve):
            w, step, sub, lanes, wf = Walk(), Count(), Count(), (Count(), Count()), Count()
            carried = [0]

            def next_use():
                dve.wait_ge(mm_done, w.use.at(1))
                return w.take("dve")

            def link(ins):
                ins.then_inc(dve_step, 1)
                step.n += 1
                settle(dve_step, step.at())

            def settle(semaphore, value):
                dve.wait_ge(semaphore, value)
                if not isinstance(value, int):
                    carried[0] += 1
                    dve.memset(carrier[:, carried[0] % 3:carried[0] % 3 + 1], 0.0)

            def inverse_root(n, width):
                u = next_use()
                dve.tensor_scalar(stat[:, 0, :], ps(u), 1.0 / width, EPS, ALU.mult, ALU.add).then_inc(dve_read, 1)
                dve.wait_ge(std_ready, n)
                link(dve.reciprocal(stat[:, 2, :], stat[:, 1, :]))
                link(dve.tensor_tensor(stat[:, 1, :], stat[:, 0, :], stat[:, 2, :], ALU.mult))
                link(dve.tensor_tensor(stat[:, 1, :], stat[:, 1, :], stat[:, 2, :], ALU.mult))
                link(dve.tensor_scalar(stat[:, 1, :], stat[:, 1, :], -0.5, 1.5, ALU.mult, ALU.add))
                link(dve.tensor_tensor(stat[:, 2, :], stat[:, 1, :], stat[:, 2, :], ALU.mult))

            def norm_x(n):
                inverse_root(n, D)
                for k in range(KD):
                    dve.tensor_tensor(H[:, k, :], X[:, k, :], stat[:, 2, :], ALU.mult).then_inc(xn_ready, 1)

            def residual(l, gate, experts):
                for k in range(KD):
                    u = None if experts else next_use()
                    for a, b, s in SEG:
                        y = ACC[:, k, a:b] if experts else ps(u)[:, a:b]
                        ins = dve.scalar_tensor_tensor(out=X[:, k, a:b], in0=y, scalar=mod[:, l, mod_at[gate] * KD + k, s:s + 1],
                                                       in1=X[:, k, a:b], op0=ALU.mult, op1=ALU.add)
                    ins.then_inc(x_ready if experts else dve_read, 1)
                dve.wait_ge(x_ready if experts else dve_read, KD * (l + 1) if experts else w.dve.at())

            def low(lane, scale):
                lanes[lane].n += 1
                dve.wait_ge(high_made[lane], lanes[lane].at())
                dve.scalar_tensor_tensor(out=parts[lane][:, 1, :], in0=raw[lane], scalar=scale, in1=parts[lane][:, 0, :],
                                         op0=ALU.mult, op1=ALU.subtract).then_inc(split[lane], 1)

            def low_part(src, dst, signal_high, signal):
                for k in range(KD):
                    dve.wait_ge(signal_high, l * KD + k + 1)
                    dve.tensor_tensor(dst[:, 1, k, :], src[:, k, :], dst[:, 0, k, :], ALU.subtract).then_inc(signal, 1)

            for i in range(2):
                dve.memset(carrier[:, i:i + 1], 0.0).then_inc(w_ready, 1)
            dve.wait_ge(vec_in, 16)
            dve.wait_ge(c_sigmoid, 1)
            flat = cact[:, :, :].rearrange("p k s -> p (k s)")
            dve.tensor_tensor(flat, flat, vecs("c"), ALU.mult).then_inc(cact_ready, 1)
            dve.wait_ge(consts_made, CONSTS)
            dve.wait_ge(x_in, 16)
            for l in range(LAYERS):
                if l == 0:
                    norm_x(1)
                    w.take("act", 2 * ADA_SLOTS)
                    ada_done = w.act.at()
                dve.wait_ge(act_read, ada_done)
                bias = vecs("b_ada")[:, l * 6 * KD:(l + 1) * 6 * KD]
                link(dve.tensor_tensor(mod[:, l, :, :], mod[:, l, :, :], bias.unsqueeze(2).to_broadcast([P, 6 * KD, 2]), ALU.add))
                for which, (sc, g) in enumerate((("sc1", "norm_mix_g"), ("sc2", "norm_ffn_g"))):
                    at = mod_at[sc] * KD
                    gv = vecs(g)[:, l * KD:(l + 1) * KD].unsqueeze(2).to_broadcast([P, KD, 2])
                    link(dve.tensor_scalar(scale[:, l, which, :, :], mod[:, l, at:at + KD, :], 1.0, None, ALU.add))
                    ins = dve.tensor_tensor(scale[:, l, which, :, :], scale[:, l, which, :, :], gv, ALU.mult)
                at = mod_at["g2"] * KD
                link(ins)
                dve.tensor_scalar(mod[:, l, at:at + KD, :], mod[:, l, at:at + KD, :], 1.0 / W_SCALE, None,
                                  ALU.mult).then_inc(mod_ready, 1)
                for lane in ((1, 0), (0, 1))[l]:
                    low(lane, U_SCALE)
                if l > 0:
                    norm_x(4)
                low_part(H, HM[l], hm_high, hm_split)
                for lane in ((1,), (0, 1, 0, 1))[l]:
                    low(lane, U_SCALE)
                if l == 0:
                    dve.wait_ge(state_in, 32)
                    w.take("act", KA)
                    for c in range(KA):
                        w.take("act")
                        dve.wait_ge(act_read, w.act.at())
                        for a, b, s in SEG:
                            o = EA_PAD * (1 + s)
                            ins = dve.tensor_tensor(EA[:, c, a + o:b + o], EA[:, c, a + o:b + o], SG[:, c % 2, a:b], ALU.mult)
                        ins.then_inc(glu_ready, 1)
                    w.take("act", 2 * KA + 2 * ADA_SLOTS)
                    ada_done = w.act.at()
                    dve.wait_ge(glu_ready, KA)
                    wide = T + EA_PAD
                    for i in range(WA):
                        for c in range(KA):
                            tap = vecs("dw_a")[:, c * WA + i:c * WA + i + 1]
                            if i == 0:
                                ins = dve.tensor_scalar(CONV[:, c, :], EA[:, c, 0:wide], tap, vecs("db_a")[:, c:c + 1],
                                                        ALU.mult, ALU.add)
                            else:
                                dve.wait_ge(dve_step, step.n - (KA - 1 if i < WA - 1 else KA - 1 - c))
                                ins = dve.scalar_tensor_tensor(out=CONV[:, c, :], in0=EA[:, c, i:i + wide], scalar=tap,
                                                               in1=CONV[:, c, :], op0=ALU.mult, op1=ALU.add)
                            if i < WA - 1:
                                ins.then_inc(dve_step, 1)
                                step.n += 1
                            else:
                                ins.then_inc(conv_ready, 1)
                    dve.wait_ge(conv_ready, KA)
                    u = next_use()
                    for k in range(KA):
                        for a, b, s in SEG:
                            ins = dve.scalar_tensor_tensor(out=YC[:, k, a:b], in0=ps(u)[:, a:b], scalar=-1.0 / DA,
                                                           in1=CONV[:, k, a + s * EA_PAD:b + s * EA_PAD],
                                                           op0=ALU.mult, op1=ALU.add)
                        ins.then_inc(centered, 1)
                    dve.wait_ge(centered, KA)
                    dve.tensor_copy(carrier[:, 3:4], ps(u, 1)).then_inc(dve_read, 1)
                    inverse_root(2, DA)
                    for k in range(KA):
                        dve.tensor_tensor(YC[:, k, :], YC[:, k, :], stat[:, 2, :], ALU.mult).then_inc(xn_ready, 1)
                    for k in range(KA):
                        dve.wait_ge(ln_sig, k + 1)
                        link(dve.tensor_scalar(YC[:, k, :], YC[:, k, :], vecs("ln_a_g")[:, k:k + 1],
                                               vecs("ln_a_b")[:, k:k + 1], ALU.mult, ALU.add))
                        dve.tensor_tensor(Z[:, k, :], YC[:, k, :], SQ[:, k, :], ALU.mult).then_inc(z_ready, 1)
                else:
                    w.take("act", KD)
                    wide = T + EC_PAD
                    first = w.act.n
                    w.take("act", KD)
                    for c in range(KD):
                        dve.wait_ge(act_read, first + c + 1)
                        u = next_use()
                        for a, b, s in SEG:
                            o = EC_PAD * (1 + s)
                            ins = dve.tensor_tensor(EC[:, c, a + o:b + o], ps(u)[:, a:b], EC[:, c, a + o:b + o], ALU.mult)
                        ins.then_inc(dve_read, 1)
                        dve.wait_ge(dve_read, w.dve.at())
                        dve.wait_ge(pads_made, 1)
                        dve.wait_ge(c_in, 16)
                        for i in range(WC):
                            tap = vecs("dw_c")[:, c * WC + i:c * WC + i + 1]
                            if i == 0:
                                link(dve.tensor_scalar(YO[:, c, 0:wide], EC[:, c, 0:wide], tap, None, ALU.mult))
                            else:
                                link(dve.scalar_tensor_tensor(out=YO[:, c, 0:wide], in0=EC[:, c, i:i + wide], scalar=tap,
                                                              in1=YO[:, c, 0:wide], op0=ALU.mult, op1=ALU.add))
                        for a, b, s in SEG:
                            o = EC_PAD * s
                            ins = dve.tensor_tensor(Z[:, c, a:b], YO[:, c, a + o:b + o], BG[:, c, a:b], ALU.mult)
                        ins.then_inc(z_ready, 1)
                residual(l, "g1", False)
                low(0, U_SCALE)
                norm_x((3, 5)[l])
                low(1, U_SCALE)
                w.take("act", NQ)
                low_part(H, H16, h_high, h_split)
                for lane in range(2):
                    low(lane, U_SCALE)

                def tile_and_steps(t, steps):
                    uu = [next_use(), next_use()]
                    settle(mm_done, w.use.at())

                    def score(q):
                        return PS[:, uu[q // 8] % PAIRS, (q % 8) * P:(q % 8 + 1) * P]

                    def best(q, lo):
                        return V16[:, q // 2, q % 2, lo:lo + 8]

                    for q in range(NQ):
                        ins = dve.max(best(q, 0), score(q))
                    link(ins)
                    for q in range(NQ):
                        dve.max_index(I16[:, q // 2, q % 2, 0:8], best(q, 0), score(q))
                        ins = dve.match_replace(ZT[:, q, :], best(q, 0), score(q), NEG)
                        if q % 8 == 7:
                            ins.then_inc(dve_read, 1)
                    settle(dve_read, w.dve.at())
                    for q in range(NQ):
                        ins = dve.max(best(q, 8), ZT[:, q, :])
                    link(ins)
                    for q in range(NQ):
                        ins = dve.max_index(I16[:, q // 2, q % 2, 8:16], best(q, 8), ZT[:, q, :])
                    link(ins)
                    shape = [P, HEADS, TOPK, TOPK]
                    link(dve.tensor_tensor(CAND.rearrange("p h (a b) -> p h a b", a=TOPK),
                                           V16[:, :, 0, :].unsqueeze(3).to_broadcast(shape),
                                           V16[:, :, 1, :].unsqueeze(2).to_broadcast(shape), ALU.add))
                    for h in range(HEADS):
                        ins = dve.max(C8[:, h, 0:8], CAND[:, h, :])
                    link(ins)
                    for h in range(HEADS):
                        dve.max_index(P8[:, h, 0:8], C8[:, h, 0:8], CAND[:, h, :])
                        ins = dve.match_replace(ZAP[:, h, :], C8[:, h, 0:8], CAND[:, h, :], NEG)
                    link(ins)
                    for h in range(HEADS):
                        ins = dve.max(C8[:, h, 8:16], ZAP[:, h, :])
                    link(ins)
                    dve.tensor_tensor(GG, C8, C8[:, :, 0:1].to_broadcast([P, HEADS, TOPK]), ALU.subtract).then_inc(shifted, 1)
                    for h in range(HEADS):
                        ins = dve.max_index(P8[:, h, 8:16], C8[:, h, 8:16], ZAP[:, h, :])
                    link(ins)
                    flat = P8.rearrange("p h k -> p (h k)")
                    dve.tensor_scalar(PLACE[:, 0, :], flat, 4, None, ALU.logical_shift_right)
                    link(dve.tensor_scalar(PLACE[:, 1, :], flat, TOPK - 1, None, ALU.bitwise_and))
                    dve.tensor_copy(IF, I16)
                    link(dve.tensor_copy(PLF, PLACE))
                    for j in range(2):
                        link(dve.tensor_tensor(PICK, PLF[:, j, :].unsqueeze(2).to_broadcast([P, P, TOPK]),
                                               iota[:, 0:TOPK].unsqueeze(1).to_broadcast([P, P, TOPK]), ALU.is_equal))
                        pick = PICK.rearrange("p (h r) a -> p h r a", h=HEADS)
                        link(dve.tensor_tensor(pick, pick, IF[:, :, j, :].unsqueeze(2).to_broadcast(shape), ALU.mult))
                        ins = dve.tensor_reduce(KEYS[:, j, :], PICK, AX.X, ALU.add)
                        if j == 0:
                            link(ins)
                    ins.then_inc(keys_found, 1)
                    dve.wait_ge(exped, t + 1)
                    link(dve.tensor_reduce(ZS, GG, AX.X, ALU.add))
                    link(dve.reciprocal(RZ, ZS))
                    dve.tensor_tensor(GG, GG, RZ.unsqueeze(2).to_broadcast([P, HEADS, TOPK]), ALU.mult).then_inc(gates_ready, 1)
                    w.take("act", 10)
                    transposed = w.act.at()
                    with loop(dve, steps, *w.steps(act=4), (sub, 4)) as turn:
                        dve.wait_ge(act_read, transposed)
                        for s in range(4):
                            tok = bass.ds(turn * STEP + SUB * s, SUB)
                            dve.wait_ge(mm_done, w.use.at(s - 3))
                            for rows, key, ready in ((O2, 1, o2_ready), (O1, 0, o1_ready)):
                                dve.tensor_tensor(rows[:, s, :, :], iota[:, :].unsqueeze(1).to_broadcast([P, SUB, P]),
                                                  IT[:, key, tok].unsqueeze(2).to_broadcast([P, SUB, P]),
                                                  ALU.is_equal).then_inc(ready, 1)
                        w.take("act", 4)
                        sub.n += 4

                with loop(dve, TILES - 1, (w.use, 28), (w.act, 26), (w.dve, 2), (sub, 16), (step, TILE_LINKS)) as turn:
                    tile_and_steps(turn + TILES * l, 4)
                tile_and_steps(TILES * l + TILES - 1, 1)
                w.take("act", 8)
                for lane in range(2):
                    lanes[lane].n += AHEAD // 2

                def gates_of(body):
                    at = slice((body % 2) * T * 8, (body % 2 + 1) * T * 8) if isinstance(body, int) else \
                        bass.ds((body % 2) * (T * 8), T * 8)
                    return GB[:, at].rearrange("p (t e) -> p t e", e=8)

                def weigh(a, gate, grp, j):
                    wf.n += 1
                    dve.tensor_tensor(a, a, gate, ALU.mult).then_inc(wf_ready, 1)
                    dve.wait_ge(wf_ready, wf.at())
                    dve.tensor_scalar(WT[:, grp, 0, j, :], a, W_SCALE, None, ALU.mult).then_inc(w_high, 1)
                    dve.wait_ge(w_high, wf.at())
                    dve.scalar_tensor_tensor(out=WT[:, grp, 1, j, :], in0=a, scalar=W_SCALE, in1=WT[:, grp, 0, j, :],
                                             op0=ALU.mult, op1=ALU.subtract).then_inc(w_ready, 1)

                def add(c):
                    dve.wait_ge(dve_read, w.dve.at(1 - KD))
                    u = next_use()
                    acc = ACC[:, c, :].rearrange("p (b c) -> p b c", b=2)
                    dve.tensor_tensor(acc, ps_halves(u), acc, ALU.add).then_inc(dve_read, 1)

                def add_and_prepare(body, lane, scale, more=True):
                    done = w.use.at()
                    for c in range(KD):
                        add(c)
                        if c == 0:
                            low(lane, scale)
                        if more and c in (1, 3, 5, 6):
                            j = (1, 3, 5, 6).index(c)
                            if j == 0:
                                dve.wait_ge(act_in[lane], act_turn(body, lane))
                                dve.wait_ge(g_in, (body + (1 - lane)) * 16 + 16 * (l * BODIES + 1))
                                dve.wait_ge(mm_done, done)
                            weigh(AB[:, lane, j, :], gates_of(body + (1 - lane))[:, :, 4 * lane + j], lane, j)

                def act_turn(body, lane):
                    return (body + (2 - lane)) * 16 + 16 * l * (AHEAD // 2)

                low(0, 1.0)
                dve.wait_ge(acc_zero, l + 1)
                dve.wait_ge(act_in[0], 16 * (l * (AHEAD // 2) + 1))
                dve.wait_ge(g_in, 16 * (l * BODIES + 1))
                for j in range(4):
                    weigh(AB[:, 0, j, :], gates_of(0)[:, :, j], 0, j)
                with loop(dve, AHEAD // 2 - 1, *w.steps(dve=16), (wf, 8), (lanes[0], 1), (lanes[1], 1)) as turn:
                    add_and_prepare(turn, 1, 1.0)
                    add_and_prepare(turn, 0, 1.0)
                add_and_prepare(AHEAD // 2 - 1, 1, 1.0)
                add_and_prepare(AHEAD // 2 - 1, 0, U_SCALE, False)

                def expert_body(turn, groups_ahead):
                    dve.wait_ge(g_in, turn * 16 + 16 * (l * BODIES + 1))
                    g = gates_of(turn)
                    for grp in range(2):
                        low(1, 1.0)
                        dve.wait_ge(mm_done, w.use.at(-8))
                        for j in range(4):
                            w.take("act")
                            dve.wait_ge(act_read, w.act.at())
                            weigh(AG[:, j % 2, :], g[:, :, 4 * grp + j], grp, j)
                        if grp < groups_ahead:
                            low(0, U_SCALE)
                        for c in range(KD):
                            add(c)

                with loop(dve, BODIES - AHEAD // 2 - 1, *w.steps(act=8, dve=16), (wf, 8), (lanes[0], 2), (lanes[1], 2)) as turn:
                    expert_body(turn + AHEAD // 2, 2)
                expert_body(BODIES - 1, 1)
                dve.wait_ge(x_back, 16 * (l + 1))
                dve.wait_ge(dve_read, w.dve.at())
                residual(l, "g2", True)
            inverse_root(6, D)
            for k in range(KD):
                dve.scalar_tensor_tensor(out=H[:, k, :], in0=X[:, k, :], scalar=vecs("final_g")[:, k:k + 1],
                                         in1=stat[:, 2, :], op0=ALU.mult, op1=ALU.mult).then_inc(y_ready, 1)


def kernel(**inputs):
    import concourse.bacc as _bacc
    from concourse.bass_utils import run_bass_kernel_spmd as _run

    x = {k: np.asarray(v) for k, v in inputs.items()}

    def chunks(a):
        n, f = a.shape
        return np.ascontiguousarray(a.T.reshape(f // P, P, n).transpose(1, 0, 2))

    def slots(wt):
        k, m = wt.shape
        return wt.reshape(k // P, P, m // 512, 512).transpose(2, 1, 0, 3).reshape(m // 512, P, SLOT)

    def u_slots(u):
        return u.reshape(GROUPS, 512, KD, P).transpose(0, 3, 2, 1).reshape(GROUPS, P, SLOT)

    def v_slots(v):
        return v.reshape(GROUPS, 4, P, D).transpose(0, 2, 1, 3).reshape(GROUPS, P, SLOT)

    cols = {
        "norm_mix_g": x["norm_mix_g"].reshape(-1, P).T,
        "norm_ffn_g": x["norm_ffn_g"].reshape(-1, P).T,
        "b_ada": x["b_ada"].reshape(-1, P).T,
        "db_a": x["db_a"].reshape(-1, P).T,
        "ln_a_g": x["ln_a_g"].reshape(-1, P).T,
        "ln_a_b": x["ln_a_b"].reshape(-1, P).T,
        "pool_scale": x["pool_scale"].reshape(-1, P).T,
        "final_g": x["final_g"].reshape(-1, P).T,
        "dw_a": chunks(x["dw_a"][0]).reshape(P, -1),
        "dw_c": chunks(x["dw_c"][0]).reshape(P, -1),
        "c": chunks(np.concatenate([x["c_prompt"], x["c_sample"]])).reshape(P, -1),
    }
    whole = [slots(w) for w in (x["w_ada"][0], x["w_ada"][1], x["w_out_even"][0], x["w_out_odd"][0])]
    split = [slots(w) for w in (x["w_in_even"][0], x["peer_wq"][0], x["w_in_odd"][0], x["peer_wq"][1])]
    keys = np.stack([x["peer_k1"], x["peer_k2"]], axis=2)
    arrays = {
        "xT": chunks(np.concatenate([x["x_prompt"][0], x["x_sample"][0]])),
        "vectors": np.concatenate([cols[name] for name, _ in VECTORS], axis=1),
        "state_a": chunks(x["state_conv_a"][0, 0]),
        "state_b": chunks(x["state_pool_b"][0, 0]),
        "state_c": chunks(x["state_conv_c"][0, 0]),
        "w_pool": x["w_pool"][0].transpose(1, 0, 2),
        "keys": keys.reshape(LAYERS, NQ, NKEYS, P).transpose(0, 3, 1, 2),
        "whole_w": np.concatenate(whole),
        "split_w": np.concatenate(split),
        "U": np.stack([u_slots(u) for u in x["peer_u"]]),
        "V": np.stack([v_slots(v) for v in x["peer_v"]]),
    }
    arrays = {k: np.ascontiguousarray(v) for k, v in arrays.items()}
    outs = {"y": (P, KD, T), "new_ap": (P, KA, EA_PAD), "new_as": (P, KA, EA_PAD), "new_bp": (P, KA, EB_PAD),
            "new_bs": (P, KA, EB_PAD), "new_cp": (P, KD, EC_PAD), "new_cs": (P, KD, EC_PAD)}
    nc = _bacc.Bacc("TRN2", target_bir_lowering=False, num_devices=1)
    args = [nc.dram_tensor(k, v.shape, F32, kind="ExternalInput").ap() for k, v in arrays.items()]
    args += [nc.dram_tensor(k, shape, F32, kind="ExternalOutput").ap() for k, shape in outs.items()]
    scratch = {"gates_dram": (P, BODIES, T, 8), "act_dram": (P, AHEAD, 4 * T), "x_dram": (P, KD * T)}
    args += [nc.dram_tensor(k, shape, F32, kind="Internal").ap() for k, shape in scratch.items()]
    build(nc, *args)
    r = _run(nc, [arrays], core_ids=[0]).results[0]

    def rows(a):
        a = np.asarray(a)
        return np.ascontiguousarray(a.transpose(2, 1, 0).reshape(a.shape[2], -1))

    y = rows(r["y"])
    new = [rows(r[k])[None, None] for k in ("new_ap", "new_bp", "new_cp", "new_as", "new_bs", "new_cs")]
    return (y[None, :NP_], y[None, NP_:], *new)
```
